# Optimizing a Trainium2 kernel written in Bass

```python
import jax, jax.numpy as jnp
from jax import lax
import numpy as np

D_MODEL = 2048
BATCH = 1
SEQ = 512
DEPTH = 1
DEC_BATCH = 8
DEC_SEQ = 8
PAST_LEN = 4096
PAGE_SIZE = 128

POOL_WIDTH = D_MODEL // 2
POOL_WINDOWS = (2, 4, 8, 16)
POOL_GROUPS = len(POOL_WINDOWS)
POOL_GROUP_DIM = POOL_WIDTH // POOL_GROUPS
POOL_BUF = max(POOL_WINDOWS) - 1
LRU_WIDTH = D_MODEL
LRU_BLOCKS = 16
LRU_BLOCK_DIM = LRU_WIDTH // LRU_BLOCKS
CONV_WIDTH = 4
CONV_BUF = CONV_WIDTH - 1
LRU_C = 8.0
IN_COLS = 2 * POOL_WIDTH + 2 * LRU_WIDTH + 2 * D_MODEL
DEEPNORM_ALPHA = (2.0 * DEPTH) ** 0.25
DEEPNORM_BETA = (8.0 * DEPTH) ** -0.25
LN_EPS = 1e-5

kernel_name = "hybrid_pool_rglru_gated_merge_step"

def _layernorm(z, g, b):
    z = z.astype(jnp.float32)
    mu = jnp.mean(z, axis=-1, keepdims=True)
    var = jnp.mean(jnp.square(z - mu), axis=-1, keepdims=True)
    return (z - mu) * lax.rsqrt(var + LN_EPS) * g + b

def _lin_combine(left, right):
    a1, b1 = left
    a2, b2 = right
    return a1 * a2, a2 * b1 + b2

def _layer(x, start, pool_buf, conv_buf, h0, w_in, b_merge, pool_w, pool_scale,
           conv_w, conv_b, lru_wa, lru_ba, lru_wx, lru_bx, lru_L,
           w_proj_a, w_proj_b, w_out, ln_g, ln_b):
    Bn, T, _ = x.shape
    f32 = jnp.float32
    proj = jnp.einsum('btd,de->bte', x, w_in)
    cuts = [POOL_WIDTH, 2 * POOL_WIDTH, 2 * POOL_WIDTH + LRU_WIDTH,
            2 * POOL_WIDTH + 2 * LRU_WIDTH, 2 * POOL_WIDTH + 2 * LRU_WIDTH + D_MODEL]
    u_a, gate_a, u_b, gate_b, m_a, m_b = jnp.split(proj, cuts, axis=-1)

    u_ext = jnp.concatenate([pool_buf.astype(u_a.dtype), u_a], axis=1)
    cs = jnp.cumsum(u_ext.astype(f32), axis=1)
    cs = jnp.pad(cs, ((0, 0), (1, 0), (0, 0)))
    pos = start + jnp.arange(T, dtype=jnp.int32)
    pooled_groups = []
    for g, w in enumerate(POOL_WINDOWS):
        lo, hi = g * POOL_GROUP_DIM, (g + 1) * POOL_GROUP_DIM
        s = (cs[:, POOL_BUF + 1:POOL_BUF + 1 + T, lo:hi]
             - cs[:, POOL_BUF + 1 - w:POOL_BUF + 1 - w + T, lo:hi])
        cnt = jnp.minimum(pos + 1, w).astype(f32)[None, :, None]
        pooled_groups.append(s / cnt)
    pooled = jnp.stack(pooled_groups, axis=2)
    diff = pooled - u_a.astype(f32).reshape(Bn, T, POOL_GROUPS, POOL_GROUP_DIM)
    mixed_a = jnp.einsum('btgc,gcd->btgd', diff, pool_w).reshape(Bn, T, POOL_WIDTH) * pool_scale
    y_a = mixed_a * jax.nn.silu(gate_a)

    xb_ext = jnp.concatenate([conv_buf.astype(u_b.dtype), u_b], axis=1)
    xc = conv_b + xb_ext[:, 0:T] * conv_w[0]
    for k in range(1, CONV_WIDTH):
        xc = xc + xb_ext[:, k:k + T] * conv_w[k]
    xcb = xc.reshape(Bn, T, LRU_BLOCKS, LRU_BLOCK_DIM)
    r = jax.nn.sigmoid(jnp.einsum('btnc,ncd->btnd', xcb, lru_wa).reshape(Bn, T, LRU_WIDTH) + lru_ba)
    i = jax.nn.sigmoid(jnp.einsum('btnc,ncd->btnd', xcb, lru_wx).reshape(Bn, T, LRU_WIDTH) + lru_bx)
    log_a = (-LRU_C * r.astype(f32)) * jax.nn.softplus(-lru_L.astype(f32))
    a = jnp.exp(log_a)
    b = jnp.sqrt(-jnp.expm1(2.0 * log_a)) * (i * xc).astype(f32)
    b = b.at[:, 0].add(a[:, 0] * h0.astype(f32))
    _, h = lax.associative_scan(_lin_combine, (a, b), axis=1)
    y_b = h * jax.nn.silu(gate_b)

    g_a = jax.nn.sigmoid(m_a + b_merge[0])
    g_b = jax.nn.sigmoid(m_b + b_merge[1])
    merged = (g_a * jnp.einsum('btc,cd->btd', y_a, w_proj_a)
              + g_b * jnp.einsum('btc,cd->btd', y_b, w_proj_b))
    out = jnp.einsum('btd,de->bte', merged, w_out)
    y = _layernorm(DEEPNORM_ALPHA * x.astype(f32) + out.astype(f32), ln_g, ln_b)
    return (y.astype(x.dtype), u_ext[:, -POOL_BUF:], xb_ext[:, -CONV_BUF:], h[:, -1])

def setup_inputs(seed: int = 0) -> dict:
    key = jax.random.key(seed)
    ks = jax.random.split(key, 24)
    nrm = lambda k, shape, s: jax.random.normal(k, shape, jnp.float32) * s
    a_base = jax.random.uniform(ks[14], (DEPTH, LRU_WIDTH), jnp.float32, 0.9, 0.999)
    sig = a_base ** (1.0 / LRU_C)
    lru_L = jnp.log(sig) - jnp.log1p(-sig)
    return {
        "x_prompt": nrm(ks[0], (BATCH, SEQ, D_MODEL), 1.0),
        "x_sample": nrm(ks[1], (DEC_BATCH, DEC_SEQ, D_MODEL), 1.0),
        "state_pool": nrm(ks[2], (DEPTH, DEC_BATCH, POOL_BUF, POOL_WIDTH), 1.0),
        "state_conv": nrm(ks[3], (DEPTH, DEC_BATCH, CONV_BUF, LRU_WIDTH), 1.0),
        "state_h": nrm(ks[4], (DEPTH, DEC_BATCH, LRU_WIDTH), 0.5),
        "w_in": nrm(ks[5], (DEPTH, D_MODEL, IN_COLS), D_MODEL ** -0.5),
        "b_merge": nrm(ks[6], (DEPTH, 2, D_MODEL), 0.02),
        "pool_w": nrm(ks[7], (DEPTH, POOL_GROUPS, POOL_GROUP_DIM, POOL_GROUP_DIM), POOL_GROUP_DIM ** -0.5),
        "pool_scale": 1.0 + nrm(ks[8], (DEPTH, POOL_WIDTH), 0.1),
        "conv_w": nrm(ks[9], (DEPTH, CONV_WIDTH, LRU_WIDTH), CONV_WIDTH ** -0.5),
        "conv_b": nrm(ks[10], (DEPTH, LRU_WIDTH), 0.02),
        "lru_wa": nrm(ks[11], (DEPTH, LRU_BLOCKS, LRU_BLOCK_DIM, LRU_BLOCK_DIM), LRU_BLOCK_DIM ** -0.5),
        "lru_ba": nrm(ks[12], (DEPTH, LRU_WIDTH), 0.02),
        "lru_wx": nrm(ks[13], (DEPTH, LRU_BLOCKS, LRU_BLOCK_DIM, LRU_BLOCK_DIM), LRU_BLOCK_DIM ** -0.5),
        "lru_bx": nrm(ks[15], (DEPTH, LRU_WIDTH), 0.02),
        "lru_L": lru_L,
        "w_proj_a": nrm(ks[16], (DEPTH, POOL_WIDTH, D_MODEL), DEEPNORM_BETA * POOL_WIDTH ** -0.5),
        "w_proj_b": nrm(ks[17], (DEPTH, LRU_WIDTH, D_MODEL), DEEPNORM_BETA * LRU_WIDTH ** -0.5),
        "w_out": nrm(ks[18], (DEPTH, D_MODEL, D_MODEL), DEEPNORM_BETA * D_MODEL ** -0.5),
        "ln_g": 1.0 + nrm(ks[19], (DEPTH, D_MODEL), 0.02),
        "ln_b": nrm(ks[20], (DEPTH, D_MODEL), 0.02),
    }

def reference(x_prompt, x_sample, state_pool, state_conv, state_h,
              w_in, b_merge, pool_w, pool_scale, conv_w, conv_b,
              lru_wa, lru_ba, lru_wx, lru_bx, lru_L,
              w_proj_a, w_proj_b, w_out, ln_g, ln_b):
    Bp = x_prompt.shape[0]
    yp, ys = x_prompt, x_sample
    pool_p, conv_p, h_p, pool_s, conv_s, h_s = [], [], [], [], [], []
    zero_pool = jnp.zeros((Bp, POOL_BUF, POOL_WIDTH), x_prompt.dtype)
    zero_conv = jnp.zeros((Bp, CONV_BUF, LRU_WIDTH), x_prompt.dtype)
    zero_h = jnp.zeros((Bp, LRU_WIDTH), jnp.float32)
    for l in range(DEPTH):
        params = (w_in[l], b_merge[l], pool_w[l], pool_scale[l], conv_w[l], conv_b[l],
                  lru_wa[l], lru_ba[l], lru_wx[l], lru_bx[l], lru_L[l],
                  w_proj_a[l], w_proj_b[l], w_out[l], ln_g[l], ln_b[l])
        yp, pb, cb, hl = _layer(yp, 0, zero_pool, zero_conv, zero_h, *params)
        pool_p.append(pb); conv_p.append(cb); h_p.append(hl)
        ys, pb, cb, hl = _layer(ys, PAST_LEN, state_pool[l], state_conv[l], state_h[l], *params)
        pool_s.append(pb); conv_s.append(cb); h_s.append(hl)
    return (yp, ys,
            jnp.stack(pool_p), jnp.stack(conv_p), jnp.stack(h_p),
            jnp.stack(pool_s), jnp.stack(conv_s), jnp.stack(h_s))


_drawn_inputs = setup_inputs


def setup_inputs(seed=0):
    import zlib

    import numpy as np

    out = dict(_drawn_inputs(seed))
    spreads = {}
    factors = {'b_merge': 8.0,
     'pool_scale': 7.027,
     'lru_ba': 8.0,
     'lru_bx': 7.555,
     'ln_g': 2.906,
     'ln_b': 2.87}
    for name, (base, spread) in spreads.items():
        noise = np.random.default_rng([zlib.crc32(name.encode()), seed]).standard_normal(out[name].shape)
        drawn = base * np.exp(spread * noise) if base else spread * noise
        out[name] = __import__('jax').numpy.asarray(drawn.astype(out[name].dtype))
    for name, factor in factors.items():
        out[name] = (out[name] * factor).astype(out[name].dtype)
    return out
```

```python
from contextlib import ExitStack

import concourse.bass as bass
from concourse import mybir

P = 128
F32 = mybir.dt.float32
F32R = mybir.dt.float32r
ALU = mybir.AluOpType
ACT = mybir.ActivationFunctionType
ds = bass.ds

INPUTS = ["x_prompt", "x_sample", "state_pool", "state_conv", "state_h", "w_in", "b_merge", "pool_w",
          "pool_scale", "conv_w", "conv_b", "lru_wa", "lru_ba", "lru_wx", "lru_bx", "lru_L",
          "w_proj_a", "w_proj_b", "w_out", "ln_g", "ln_b"]


def build(nc, a, host, out):
    SEQ, D = a["x_prompt"].shape[1:]
    NSEQ, NEW = a["x_sample"].shape[:2]
    HIST, PW = a["state_pool"].shape[2:]
    CH = a["state_conv"].shape[2]
    TAPS = CH + 1
    GROUPS = a["pool_w"].shape[1]
    GD = PW // GROUPS
    SAMP = NSEQ * NEW
    T = SEQ + SAMP
    TH = T // 2
    DT, PT_ = D // P, PW // P
    BLOCKS = a["lru_wa"].shape[1]
    CK = 4
    RING = 4
    WIDTHS = (2, 4, 8, 16)
    ALPHA = 2.0 ** 0.25
    EPS = 1e-5
    XT = SEQ // P
    PSEG, CSEG = HIST + NEW, CH + NEW
    PEXT = HIST + SEQ + NSEQ * PSEG
    CEXT = CH + SEQ + NSEQ * CSEG
    XE = CEXT - CH
    XEH = XE // 2
    SROWS = 1 + NSEQ
    PROWS, CROWS = HIST + SAMP, CH * SROWS

    COL_UA, COL_GA, COL_UB = 0, PW, 2 * PW
    COL_GB, COL_MA = COL_UB + D, COL_UB + 2 * D
    COL_MB = COL_MA + D
    PER_GATE, PER_POOL, PER_PROJA, PER_LRU, PER_PROJB, PER_OUT = 8, 16, 12, 8, 8, 8
    Q_GATE = 0
    Q_POOL = Q_GATE + DT // 2 * PER_GATE
    Q_PROJA = Q_POOL + GROUPS * PER_POOL
    Q_LRU = Q_PROJA + DT // 2 * PER_PROJA
    Q_PROJB = Q_LRU + BLOCKS * PER_LRU
    Q_OUT = Q_PROJB + DT // 2 * PER_PROJB
    Q_END = Q_OUT + DT // 2 * PER_OUT

    x_prompt = a["x_prompt"][0].rearrange("(t p) d -> t p d", p=P)
    x_sample = a["x_sample"].rearrange("b s d -> (b s) d")
    y_prompt = out[0][0].rearrange("(t p) d -> t p d", p=P)
    y_sample = out[1].rearrange("b s d -> (b s) d")
    w_in, w_pa, w_pb, w_out = a["w_in"][0], a["w_proj_a"][0], a["w_proj_b"][0], a["w_out"][0]
    gate_b_dram = nc.dram_tensor("gate_b_scratch", (DT, P, T), F32, kind="Internal").ap()
    part_a_dram = nc.dram_tensor("part_a_scratch", (DT, P, T), F32, kind="Internal").ap()
    DVE_TILES, POOL_TILES = (0, 1, 2, 4), (3,)
    ROW_STORES = NSEQ + 7
    STORES = 1 + XT + 1
    XBLOCKS = DT // CK
    X_BANKS = XBLOCKS * (XT + 1)
    SETUP_BANKS = X_BANKS + 5

    with ExitStack() as ctx:
        def sem(name):
            return ctx.enter_context(nc.semaphore(name))

        def alloc(stack, name, shape, dt=F32):
            return stack.enter_context(nc.sbuf_tensor(name, shape, dt))

        xh = alloc(ctx, "xh", [P, DT, T], F32R)
        xl = alloc(ctx, "xl", [P, DT, T], F32R)
        weight_raw = alloc(ctx, "weight_raw", [P, RING, CK, P])
        weight_hi = alloc(ctx, "weight_hi", [P, RING, CK, P], F32R)
        weight_lo = alloc(ctx, "weight_lo", [P, RING, CK, P], F32R)
        ident = alloc(ctx, "ident", [P, P])
        counts = alloc(ctx, "counts", [P, HIST])
        chan = alloc(ctx, "chan", [P, 8 * DT])
        bias_m = alloc(ctx, "bias_m", [P, 2 * DT + PT_])
        bias_ri = alloc(ctx, "bias_ri", [P, 2 * DT])
        neg_c2 = alloc(ctx, "neg_c2", [P, DT])
        pos_c4 = alloc(ctx, "pos_c4", [P, DT])
        conv_hist = alloc(ctx, "conv_hist", [P, DT, NSEQ * CH])
        h_init = alloc(ctx, "h_init", [P, DT, NSEQ])
        pool_rows = alloc(ctx, "pool_rows", [P, PROWS, PT_])
        conv_rows = alloc(ctx, "conv_rows", [P, CROWS, DT])
        h_rows = alloc(ctx, "h_rows", [P, SROWS, DT])
        start_term = alloc(ctx, "start_term", [P, NSEQ])
        CONV_W, CONV_B, LRU_BA, LRU_BX, LRU_L = 0, TAPS * DT, (TAPS + 1) * DT, (TAPS + 2) * DT, (TAPS + 3) * DT

        with ExitStack() as s:
            x_rows = alloc(s, "x_rows", [P, XT + 1, D])
            conv_state = alloc(s, "conv_state", [NSEQ * CH, D])
            h_state = alloc(s, "h_state", [NSEQ, D])
            pool_state = alloc(s, "pool_state", [NSEQ * HIST, PW])
            chan_rows = alloc(s, "chan_rows", [P, P])
            bias_rows = alloc(s, "bias_rows", [2 * DT + PT_, P])
            sp = [alloc(s, f"softplus{i}", [P, DT]) for i in range(5)]
        with ExitStack() as s:
            yah = alloc(s, "yah", [P, PT_, T], F32R)
            yal = alloc(s, "yal", [P, PT_, T], F32R)
            pool_ext = [alloc(s, f"pool_ext{i}", [P, PEXT]) for i in range(2)]
            window = [alloc(s, f"window{i}", [P, PEXT]) for i in range(2)]
            diff = alloc(s, "diff", [P, T])
            dfh = alloc(s, "dfh", [P, 2, T], F32R)
            dfl = alloc(s, "dfl", [P, 2, T], F32R)
            pool_tanh = alloc(s, "pool_tanh", [P, T])
            pool_silu = [alloc(s, f"pool_silu{i}", [P, T]) for i in range(2)]
            y_a = alloc(s, "y_a", [P, T])
        with ExitStack() as s:
            ybh = alloc(s, "ybh", [P, DT, T], F32R)
            ybl = alloc(s, "ybl", [P, DT, T], F32R)
        with ExitStack() as s:
            z = alloc(s, "z", [P, XT + 1, D])
            gamma = alloc(s, "gamma", [P, D])
            beta = alloc(s, "beta", [P, D])
            out_sb = [alloc(s, f"out_sb{i}", [P, T]) for i in range(2)]
            stats = alloc(s, "stats", [P, XT + 1, DT, 6])
            moments = alloc(s, "moments", [P, XT + 1, 2])
            rstd = [alloc(s, f"rstd{i}", [P, XT + 1]) for i in range(4)]
        big = ctx.enter_context(nc.sbuf_tensor("big_region", [P, 2 * DT * T], F32))
        with ExitStack() as s:
            conv_x_hi = alloc(s, "conv_x_hi", [P, CEXT], F32R)
            conv_x_lo = alloc(s, "conv_x_lo", [P, CEXT], F32R)
            conv_ext = alloc(s, "conv_ext", [P, CEXT])
            r_tanh = alloc(s, "r_tanh", [P, CEXT])
            small_raw = alloc(s, "small_raw", [P, 2, P])
            small_hi = alloc(s, "small_hi", [P, 2, P], F32R)
            small_lo = alloc(s, "small_lo", [P, 2, P], F32R)
            i_tanh = alloc(s, "i_tanh", [P, CEXT])
            decay = alloc(s, "decay", [P, CEXT])
            half_tanh = alloc(s, "half_tanh", [P, CEXT])
            root = alloc(s, "root", [P, CEXT])
            conv_x = alloc(s, "conv_x", [P, CEXT])
            gb_tanh = alloc(s, "gb_tanh", [P, T])
            gb_silu = alloc(s, "gb_silu", [P, T])
        with ExitStack() as s:
            gate_out = [alloc(s, f"gate_out{i}", [P, T]) for i in range(2)]
            ma_tanh = [alloc(s, f"ma_tanh{i}", [P, T]) for i in range(2)]
            part_out = [alloc(s, f"part_out{i}", [P, T]) for i in range(2)]
            pool_hist = alloc(s, "pool_hist", [P, PT_, NSEQ * HIST])
            pw_raw = alloc(s, "pw_raw", [P, 2, GD])
            pw_hi = alloc(s, "pw_hi", [P, 2, GD], F32R)
            pw_lo = alloc(s, "pw_lo", [P, 2, GD], F32R)
        with ExitStack() as s:
            gate_in = [alloc(s, f"gate_in{i}", [P, T]) for i in range(2)]
            part_in = [alloc(s, f"part_in{i}", [P, T]) for i in range(2)]
            alloc(s, "below_merged", [P, 876])
            merged = alloc(s, "merged", [P, T])
            rows_sb = alloc(s, "rows_sb", [P, 3, 4 * P])
        ps = ctx.enter_context(nc.psum_tensor("ps", [P, 8, 512], F32))

        def pair(i, n=TH):
            return ps[:, 2 * i:2 * i + 2, 0:n]

        def halves(ap):
            return ap.rearrange("p (h n) -> p h n", h=2)

        def f32(ap):
            return ap.bitcast(F32)

        def conv_seg(buf, off, n):
            v = buf[:, CH + SEQ:CH + SEQ + NSEQ * CSEG].rearrange("p (b s) -> p b s", s=CSEG)
            return v[:, :, off:off + n]

        def pool_seg(buf, off, n):
            v = buf[:, HIST + SEQ:HIST + SEQ + NSEQ * PSEG].rearrange("p (b s) -> p b s", s=PSEG)
            return v[:, :, off:off + n]

        def sample_cols(ap):
            return ap.rearrange("p (b s) -> p b s", s=NEW)

        def gate_col(which, m):
            return bias_m[:, ds(which * DT + m, 1)]

        raw_landed = [sem(f"raw_landed{i}") for i in range(RING)]
        weight_hi_ready, weight_lo_ready, chunk_done = sem("weight_hi_ready"), sem("weight_lo_ready"), sem("chunk_done")
        x_landed = [sem(f"x_landed{i}") for i in range(XBLOCKS)]
        ident_landed, consts_landed, states_landed = sem("ident_landed"), sem("consts_landed"), sem("states_landed")
        setup_turned, setup_hi, setup_taken = sem("setup_turned"), sem("setup_hi"), sem("setup_taken")
        param_step, param_exp, params_ready = sem("param_step"), sem("param_exp"), sem("params_ready")
        pads_zero = sem("pads_zero")
        gate_tanh_ready = sem("gate_tanh_ready")
        gate_spilled = [sem(f"gate_spilled{i}") for i in range(2)]
        hist_in, ext_ready, rows_kept = sem("pool_hist_in"), sem("pool_ext_ready"), sem("pool_rows_kept")
        window_step, diff_ready, diff_hi, diff_lo = sem("window_step"), sem("diff_ready"), sem("diff_hi"), sem("diff_lo")
        pw_landed, pw_hi_ready, pw_lo_ready, mixed_done = sem("pw_landed"), sem("pw_hi_ready"), sem("pw_lo_ready"), sem("mixed_done")
        pool_tanh_ready, pool_silu_ready, ya_ready, ya_hi, ya_lo = (
            sem("pool_tanh_ready"), sem("pool_silu_ready"), sem("ya_ready"), sem("ya_hi"), sem("ya_lo"))
        ma_tanh_ready, part_ready = sem("ma_tanh_ready"), sem("part_ready")
        part_spilled = [sem(f"part_spilled{i}") for i in range(2)]
        conv_hist_in, conv_ext_ready, conv_rows_kept = sem("conv_hist_in"), sem("conv_ext_ready"), sem("conv_rows_kept")
        tap_done = [sem(f"tap_done{i}") for i in range(TAPS)]
        conv_hi, conv_lo = sem("conv_hi"), sem("conv_lo")
        small_landed, small_hi_ready, small_lo_ready, lru_done = (
            sem("small_landed"), sem("small_hi_ready"), sem("small_lo_ready"), sem("lru_done"))
        gb_tanh_ready, gb_silu_ready, r_ready, i_ready = sem("gb_tanh_ready"), sem("gb_silu_ready"), sem("r_ready"), sem("i_ready")
        exp_ready, half_ready, root_ready = sem("exp_ready"), sem("half_ready"), sem("root_ready")
        ix_ready, fall_ready, decay_ready, scale_ready, drive_ready = (
            sem("ix_ready"), sem("fall_ready"), sem("decay_ready"), sem("scale_ready"), sem("drive_ready"))
        start_ready, decay_cut, h_ready, h_kept = sem("start_ready"), sem("decay_cut"), sem("h_ready"), sem("h_kept")
        yb_ready, yb_hi, yb_lo = sem("yb_ready"), sem("yb_hi"), sem("yb_lo")
        gate_loaded = [sem(f"gate_loaded{i}") for i in range(2)]
        gated_ready, merge_ready, merged_hi, merged_lo = sem("gated_ready"), sem("merge_ready"), sem("merged_hi"), sem("merged_lo")
        rows_turned, rows_ready = sem("rows_turned"), sem("rows_ready")
        z_loaded, moments_ready, shift_ready = sem("z_loaded"), sem("moments_ready"), sem("shift_ready")
        pool_scaled, pool_normed = sem("pool_scaled"), sem("pool_normed")
        out_copied, out_turned, z_added, z_stats = sem("out_copied"), sem("out_turned"), sem("z_added"), sem("z_stats")
        norm_step, root_var, centred, normed = sem("norm_step"), sem("root_var"), sem("centred"), sem("normed")
        stored, rows_stored = sem("stored"), sem("rows_stored")

        block = ctx.enter_context(nc.Block())

        def wait(eng, s, value):
            if isinstance(value, int) and value <= 0:
                return
            eng.wait_ge(s, value)

        def rounds(i, per, q0):
            return i * (per // RING) + q0 // RING

        def setup_bank(s):
            return ps[:, 4 + s % 4]

        def x_step(s):
            c, t = divmod(s, XT + 1)
            return c, t, P if t < XT else SAMP

        TURNED_BEFORE = [9, 13, 17] + [X_BANKS] * (PER_GATE - 3)
        SPLIT_BEFORE = [5, 9, 13, 17] + [X_BANKS] * (PER_GATE - 4)

        def setup_order(x_bank, chunk, before):
            done = 0
            for q in range(PER_GATE):
                for s in range(done, before[q]):
                    x_bank(s)
                done = before[q]
                chunk(q)

        PROJB_FIRST = [(m, c) for m in range(2) for c in range(DT // CK - 1)] + [(m, DT // CK - 1) for m in range(2)]

        def store(eng, t):
            if t < XT:
                eng.dma_start(y_prompt[t], z[:, t]).then_inc(stored, 16)
            else:
                eng.dma_start(y_sample, z[0:SAMP, t]).then_inc(stored, 16)

        @block.sync
        def _(sync):
            def tile(w, m, r, j, base=0, rows=D, paired=0):
                w = w[:, base:base + min(w.shape[1] - base, D)].rearrange("k (m n) -> k m n", n=P)
                for k in range(j, j + rows // (CK * P)):
                    if paired and k % 2 and k + 1 < paired:
                        wait(sync, weight_lo_ready, r * RING + (k + 2 - RING))
                    elif not paired or k % 2 or k == 0:
                        wait(sync, weight_lo_ready, r * RING + (k + 1 - RING))
                    sync.dma_start(weight_raw[:, k % RING],
                                   w[(k - j) * CK * P:(k - j + 1) * CK * P, ds(m, 1), :].rearrange("(c p) o n -> p c (o n)", p=P))\
                        .then_inc(raw_landed[k % RING], 16)

            def load_x(c):
                cols = slice(c * CK * P, (c + 1) * CK * P)
                sync.dma_start(x_rows[:, 0:XT, cols], a["x_prompt"][0][:, cols].rearrange("(t p) d -> p t d", p=P)).then_inc(x_landed[c], 16)
                sync.dma_start(x_rows[0:SAMP, XT, cols], x_sample[:, cols]).then_inc(x_landed[c], 16)

            def load_chunk(q):
                c, m = divmod(q, 2)
                wait(sync, weight_lo_ready, q + 1 - RING)
                sync.dma_start(weight_raw[:, q % RING],
                               w_in[c * CK * P:(c + 1) * CK * P, COL_MB + m * P:COL_MB + (m + 1) * P].rearrange("(c p) n -> p c n", p=P))\
                    .then_inc(raw_landed[q % RING], 16)

            def gate(i):
                for m in range(2):
                    tile(w_in, i * 2 + m, rounds(i, PER_GATE, Q_GATE), 4 * m, COL_MB)

            load_x(0)
            for q in range(PER_GATE):
                load_chunk(q)
                if q in (0, 1, 3):
                    load_x(q // 2 + 1 + q % 2)
            sync.dma_start(conv_state[:, :], a["state_conv"][0].rearrange("b s d -> (b s) d")).then_inc(states_landed, 16)
            sync.dma_start(h_state[:, :], a["state_h"][0]).then_inc(states_landed, 16)
            sync.dma_start(pool_state[:, :], a["state_pool"][0].rearrange("b s d -> (b s) d")).then_inc(states_landed, 16)
            sync.dma_start(out[5][0][:, 0:HIST - NEW, :], a["state_pool"][0][:, NEW:, :]).then_inc(stored, 16)
            with sync.Fori(1, DT // 2) as i:
                gate(i)
            with sync.Fori(0, GROUPS) as g:
                for n, part in enumerate((COL_UA, COL_UA + P, COL_GA, COL_GA + P)):
                    tile(w_in, g * (GD // P), rounds(g, PER_POOL, Q_POOL), 4 * n, part)
            with sync.Fori(0, DT // 2) as i:
                for m in range(2):
                    tile(w_in, i * 2 + m, rounds(i, PER_PROJA, Q_PROJA), 4 * m, COL_MA, paired=PER_PROJA)
                for m in range(2):
                    tile(w_pa, i * 2 + m, rounds(i, PER_PROJA, Q_PROJA), 8 + 2 * m, rows=PW, paired=PER_PROJA)
            with sync.Fori(0, BLOCKS) as n:
                tile(w_in, n, rounds(n, PER_LRU, Q_LRU), 0, COL_UB)
                tile(w_in, n, rounds(n, PER_LRU, Q_LRU), 4, COL_GB)
            for j, (m, c) in enumerate(PROJB_FIRST):
                wait(sync, weight_lo_ready, Q_PROJB + j + 1 - RING)
                sync.dma_start(weight_raw[:, j % RING],
                               w_pb[c * CK * P:(c + 1) * CK * P, m * P:(m + 1) * P].rearrange("(c p) n -> p c n", p=P))\
                    .then_inc(raw_landed[j % RING], 16)
            for w, q0, first in ((w_pb, Q_PROJB, 1), (w_out, Q_OUT, 0)):
                with sync.Fori(first, DT // 2) as i:
                    for m in range(2):
                        tile(w, i * 2 + m, rounds(i, 8, q0), 4 * m)
            for n, t in enumerate(DVE_TILES):
                sync.wait_ge(normed, n + 1)
                store(sync, t)
            sync.wait_ge(stored, 16 * STORES)
            sync.wait_ge(rows_stored, 16 * ROW_STORES)

        @block.gpsimd
        def _(pool):
            def spill(m, slot, src, ready, dram, done):
                pool.wait_ge(ready, m + 1)
                pool.wait_ge(params_ready, 1)
                pool.dma_start(dram[ds(m, 1)].rearrange("o p n -> (o p) n"), src[slot][:, :]).then_inc(done[slot], 16)

            with pool.Fori(0, DT // 2) as i:
                for m in range(2):
                    spill(i * 2 + m, m, gate_out, gate_tanh_ready, gate_b_dram, gate_spilled)

            pool.wait_ge(setup_taken, SETUP_BANKS)
            for b in pool_ext:
                pool.memset(b[:, 0:HIST], 0.0).then_inc(pads_zero, 1)

            def pool_group(g):
                wait(pool, pw_lo_ready, g)
                pool.wait_ge(params_ready, 1)
                pool.dma_start(pw_raw[:], a["pool_w"][0][ds(g, 1)].rearrange("o (k p) n -> p (o k) n", p=P))\
                    .then_inc(pw_landed, 16)
                for u in range(2):
                    wait(pool, diff_ready, g * 2 + (u - 1))
                    wait(pool, rows_kept, g * 2 + (u - 1))
                    pool.wait_ge(params_ready, 1)
                    pool.tensor_copy(pool_seg(pool_ext[u], 0, HIST),
                                     pool_hist[:, ds(g * 2 + u, 1), :].rearrange("p o (b s) -> p (o b) s", s=HIST))\
                        .then_inc(hist_in, 1)
                for u in range(2):
                    pool.wait_ge(ext_ready, g * 2 + (u + 1))
                    pool.wait_ge(params_ready, 1)
                    kept = pool_rows[:, :, ds(g * 2 + u, 1)]
                    pool.tensor_copy(kept[:, 0:HIST], pool_ext[u][:, SEQ:SEQ + HIST].rearrange("p (s o) -> p s o", o=1))
                    pool.tensor_copy(kept[:, HIST:].rearrange("p (b s) o -> p b (s o)", s=NEW),
                                     pool_seg(pool_ext[u], HIST, NEW)).then_inc(rows_kept, 1)

            pool_group(0)
            with pool.Fori(1, GROUPS) as g:
                pool_group(g)

            with pool.Fori(0, DT // 2) as i:
                for m in range(2):
                    spill(i * 2 + m, m, part_out, part_ready, part_a_dram, part_spilled)

            for s in (*gate_spilled, *part_spilled):
                pool.wait_ge(s, 16 * DT // 2)
            pool.memset(conv_ext[:, 0:CH], 0.0).then_inc(pads_zero, 1)

            def keep_h(n):
                pool.wait_ge(h_ready, n + 1)
                pool.wait_ge(params_ready, 1)
                kept = h_rows[:, :, ds(n, 1)]
                pool.tensor_copy(kept[:, 0:1], half_tanh[:, SEQ - 1:SEQ].rearrange("p (s o) -> p s o", o=1))
                pool.tensor_copy(kept[:, 1:SROWS], conv_seg(half_tanh, NEW - 1, 1)).then_inc(h_kept, 1)

            def lru_block(n, before):
                wait(pool, small_lo_ready, n)
                pool.wait_ge(params_ready, 1)
                for k, w in enumerate((a["lru_wa"], a["lru_wx"])):
                    pool.dma_start(small_raw[:, k], w[0][ds(n, 1)].rearrange("o p n -> (o p) n"))\
                        .then_inc(small_landed, 16)
                wait(pool, tap_done[TAPS - 1], n)
                wait(pool, conv_rows_kept, n)
                pool.wait_ge(params_ready, 1)
                pool.tensor_copy(conv_seg(conv_ext, 0, CH),
                                 conv_hist[:, ds(n, 1), :].rearrange("p o (b s) -> p (o b) s", s=CH))\
                    .then_inc(conv_hist_in, 1)
                if before is not None:
                    keep_h(before)
                pool.wait_ge(conv_ext_ready, n + 1)
                pool.wait_ge(params_ready, 1)
                kept = conv_rows[:, :, ds(n, 1)]
                pool.tensor_copy(kept[:, 0:CH], conv_ext[:, SEQ:SEQ + CH].rearrange("p (s o) -> p s o", o=1))
                pool.tensor_copy(kept[:, CH:].rearrange("p (b s) o -> p b (s o)", s=CH),
                                 conv_seg(conv_ext, NEW, CH)).then_inc(conv_rows_kept, 1)

            lru_block(0, None)
            with pool.Fori(1, BLOCKS) as n:
                lru_block(n, n - 1)

            keep_h(BLOCKS - 1)
            pool.wait_ge(lru_done, BLOCKS)
            pool.wait_ge(conv_rows_kept, BLOCKS)
            pool.wait_ge(half_ready, BLOCKS)

            def merge_inputs(i):
                for m in range(2):
                    wait(pool, merge_ready, i * 2 + (m - 1))
                    pool.wait_ge(params_ready, 1)
                    pool.dma_start(gate_in[m][:, :], gate_b_dram[ds(i * 2 + m, 1)].rearrange("o p n -> (o p) n"))\
                        .then_inc(gate_loaded[m], 16)
                    pool.dma_start(part_in[m][:, :], part_a_dram[ds(i * 2 + m, 1)].rearrange("o p n -> (o p) n"))\
                        .then_inc(gate_loaded[m], 16)

            merge_inputs(0)
            merge_inputs(1)
            pool.wait_ge(rows_ready, 3)
            rows = lambda b, c: rows_sb[:, b, c * P:(c + 1) * P]
            per = P // PT_ // NEW
            pool_new = out[5][0][:, HIST - NEW:, :].rearrange("b s (j p) -> b s j p", p=P)
            for b in range(NSEQ):
                src = rows(0, b // per)[b % per * NEW * PT_:(b % per + 1) * NEW * PT_, :]
                pool.dma_start(pool_new[b].rearrange("s j p -> (s j) p"), src).then_inc(rows_stored, 16)
            pool.dma_start(out[2][0].rearrange("b s (j p) -> (b s j) p", p=P), rows(1, 0)[0:HIST * PT_, :]).then_inc(rows_stored, 16)
            pool.dma_start(out[4][0].rearrange("b (j p) -> (b j) p", p=P), rows(1, 1)[0:DT, :]).then_inc(rows_stored, 16)
            pool.dma_start(out[7][0].rearrange("b (j p) -> (b j) p", p=P), rows(1, 2)[0:NSEQ * DT, :]).then_inc(rows_stored, 16)
            pool.dma_start(out[3][0].rearrange("b s (j p) -> (b s j) p", p=P), rows(2, 3)[0:CH * DT, :]).then_inc(rows_stored, 16)
            conv_new = out[6][0].rearrange("b s (j p) -> (b s j) p", p=P)
            for c in range(3):
                pool.dma_start(conv_new[c * P:(c + 1) * P, :], rows(2, c)).then_inc(rows_stored, 16)
            with pool.Fori(2, DT // 2) as i:
                merge_inputs(i)

            pool.wait_ge(chunk_done, Q_OUT)
            for t in range(XT):
                pool.dma_start(z[:, t], x_prompt[t]).then_inc(z_loaded, 16)
            pool.dma_start(z[0:SAMP, XT], x_sample).then_inc(z_loaded, 16)
            pool.dma_start(gamma[:, :], a["ln_g"].partition_broadcast(P)).then_inc(z_loaded, 16)
            pool.dma_start(beta[:, :], a["ln_b"].partition_broadcast(P)).then_inc(z_loaded, 16)
            for n, t in enumerate(POOL_TILES):
                pool.wait_ge(centred, n + 1)
                pool.tensor_tensor(z[:, t], z[:, t], gamma[:, :], ALU.mult).then_inc(pool_scaled, 1)
                pool.wait_ge(pool_scaled, n + 1)
                pool.tensor_tensor(z[:, t], z[:, t], beta[:, :], ALU.add).then_inc(pool_normed, 1)

        @block.scalar
        def _(act):
            def split(r, j):
                act.wait_ge(raw_landed[j % RING], r * 16 + 16 * (j // RING + 1))
                wait(act, chunk_done, r * RING + (j + 1 - RING))
                act.activation(weight_hi[:, j % RING], weight_raw[:, j % RING], ACT.Copy).then_inc(weight_hi_ready, 1)

            def steps(r, per, tail, own, last=False):
                for j in range(per):
                    if not (last and j + 3 >= per):
                        split(r, j + 3)
                    tail(j)
                    own(j)

            act.dma_start(ident[:, :], host["identity"]).then_inc(ident_landed, 16)
            act.dma_start(counts[:, :], host["reciprocals"]).then_inc(consts_landed, 16)
            for row, name in ((CONV_W, "conv_w"), (CONV_B, "conv_b"), (LRU_BA, "lru_ba"), (LRU_BX, "lru_bx"), (LRU_L, "lru_L")):
                v = a[name].rearrange("o (n p) -> (o n) p", p=P) if len(a[name].shape) == 2 else \
                    a[name].rearrange("o k (n p) -> (o k n) p", p=P)
                act.dma_start(chan_rows[row:row + v.shape[0], :], v).then_inc(consts_landed, 16)
            act.dma_start(bias_rows[0:2 * DT, :], a["b_merge"].rearrange("o k (n p) -> (o k n) p", p=P)).then_inc(consts_landed, 16)
            act.dma_start(bias_rows[2 * DT:, :], a["pool_scale"].rearrange("o (n p) -> (o n) p", p=P)).then_inc(consts_landed, 16)
            def round_x(s):
                c, t, n = x_step(s)
                act.wait_ge(setup_turned, s + 1)
                act.activation(xh[:, CK * c:CK * c + CK, t * P:t * P + n],
                               setup_bank(s)[:, 0:CK * n].rearrange("p (k n) -> p k n", n=n), ACT.Copy).then_inc(setup_hi, 1)

            setup_order(round_x, lambda q: split(0, q), SPLIT_BEFORE)
            act.wait_ge(param_step, 1)
            act.activation(sp[1][:, :], sp[0][:, :], ACT.Exp, scale=-1.0).then_inc(param_exp, 1)
            for j in range(RING - 1):
                split(0, PER_GATE + j)

            def gate_tanh(i, m, r, j):
                act.wait_ge(chunk_done, r * RING + j)
                wait(act, gate_spilled[m], i * 16)
                act.wait_ge(params_ready, 1)
                act.activation(halves(gate_out[m][:, :]), pair(m), ACT.Tanh, bias=gate_col(1, i * 2 + m), scale=0.5)\
                    .then_inc(gate_tanh_ready, 1)

            def gate_tail(i, r):
                def tail(j):
                    if j == 0:
                        gate_tanh(i, 1, r, 0)
                return tail

            def gate(i, tail):
                r = rounds(i, PER_GATE, Q_GATE)
                steps(r, PER_GATE, tail, lambda j: gate_tanh(i, 0, r, 4) if j == 4 else None)

            gate_tanh(0, 0, 0, PER_GATE - 1)
            with act.Fori(1, DT // 2) as i:
                gate(i, gate_tail(i - 1, rounds(i, PER_GATE, Q_GATE)))

            def pool_copy(g, u, r):
                e = pool_ext[u]
                act.wait_ge(chunk_done, r * RING + 4 * (u + 1))
                act.wait_ge(hist_in, g * 2 + (u + 1))
                act.activation(e[:, HIST:HIST + TH], ps[:, 2 * u, 0:TH], ACT.Copy)
                act.activation(e[:, HIST + TH:HIST + SEQ], ps[:, 2 * u + 1, 0:SEQ - TH], ACT.Copy)
                act.activation(pool_seg(e, HIST, NEW), sample_cols(ps[:, 2 * u + 1, SEQ - TH:TH]), ACT.Copy)\
                    .then_inc(ext_ready, 1)

            def diff_round(g, u):
                act.wait_ge(diff_ready, g * 2 + (u + 1))
                wait(act, mixed_done, g * 2)
                act.activation(dfh[:, u], diff[:, :], ACT.Copy).then_inc(diff_hi, 1)

            def pool_tanh_of(g, u, r, j):
                act.wait_ge(chunk_done, r * RING + j)
                wait(act, pool_silu_ready, g * 2 + u)
                act.activation(halves(pool_tanh[:, :]), pair(2 + u), ACT.Tanh, scale=0.5).then_inc(pool_tanh_ready, 1)

            def ya_round(g, u):
                act.wait_ge(ya_ready, g * 2 + (u + 1))
                act.wait_ge(params_ready, 1)
                act.activation(yah[:, ds(g * 2 + u, 1), :].rearrange("p o n -> p (o n)"), y_a[:, :], ACT.Copy).then_inc(ya_hi, 1)

            def pool_tail(g, r):
                def tail(j):
                    if j == 0:
                        pool_tanh_of(g, 1, r, 0)
                    if j == 2:
                        ya_round(g, 1)
                return tail

            def pool_group(g, tail):
                r = rounds(g, PER_POOL, Q_POOL)

                def own(j):
                    if j == 4:
                        pool_copy(g, 0, r)
                    if j == 6:
                        diff_round(g, 0)
                    if j == 7:
                        act.wait_ge(pw_landed, g * 16 + 16)
                        wait(act, mixed_done, g * 2)
                        act.activation(pw_hi[:], pw_raw[:], ACT.Copy).then_inc(pw_hi_ready, 1)
                    if j == 8:
                        pool_copy(g, 1, r)
                    if j == 10:
                        diff_round(g, 1)
                    if j == 12:
                        pool_tanh_of(g, 0, r, 12)
                    if j == 14:
                        ya_round(g, 0)
                steps(r, PER_POOL, tail, own)

            pool_group(0, gate_tail(DT // 2 - 1, Q_POOL // RING))
            with act.Fori(1, GROUPS) as g:
                pool_group(g, pool_tail(g - 1, rounds(g, PER_POOL, Q_POOL)))

            def proj_a(i, tail):
                r = rounds(i, PER_PROJA, Q_PROJA)

                def own(j):
                    if j in (4, 8):
                        m = j // 4 - 1
                        act.wait_ge(chunk_done, r * RING + j)
                        wait(act, part_ready, i * 2 + (m - 1))
                        act.wait_ge(params_ready, 1)
                        act.activation(halves(ma_tanh[m][:, :]), pair(m), ACT.Tanh, bias=gate_col(0, i * 2 + m), scale=0.5)\
                            .then_inc(ma_tanh_ready, 1)
                steps(r, PER_PROJA, tail, own)

            proj_a(0, pool_tail(GROUPS - 1, Q_PROJA // RING))
            with act.Fori(1, DT // 2) as i:
                proj_a(i, lambda j: None)

            def lru_tail(n, r):
                def tail(j):
                    if j == 0:
                        act.wait_ge(chunk_done, r * RING)
                        wait(act, yb_lo, n)
                        act.activation(halves(gb_tanh[:, :]), pair(1), ACT.Tanh, scale=0.5).then_inc(gb_tanh_ready, 1)
                        act.wait_ge(lru_done, n + 1)
                        act.wait_ge(params_ready, 1)
                        act.activation(r_tanh[:, 0:XE].rearrange("p (h n) -> p h n", h=2), pair(2, XEH), ACT.Tanh,
                                       bias=bias_ri[:, ds(n, 1)], scale=0.5).then_inc(r_ready, 1)
                        wait(act, h_ready, n)
                        act.wait_ge(params_ready, 1)
                        act.activation(i_tanh[:, 0:XE].rearrange("p (h n) -> p h n", h=2), pair(3, XEH), ACT.Tanh,
                                       bias=bias_ri[:, ds(n + DT, 1)], scale=0.5).then_inc(i_ready, 1)
                    if j == 1:
                        act.wait_ge(r_ready, n + 1)
                        act.wait_ge(params_ready, 1)
                        act.activation(decay[:, 0:XE], r_tanh[:, 0:XE], ACT.Exp,
                                       bias=neg_c2[:, ds(n, 1)], scale=neg_c2[:, ds(n, 1)]).then_inc(exp_ready, 1)
                        wait(act, yb_ready, n)
                        wait(act, h_kept, n)
                        act.wait_ge(params_ready, 1)
                        act.activation(half_tanh[:, 0:XE], r_tanh[:, 0:XE], ACT.Tanh,
                                       bias=pos_c4[:, ds(n, 1)], scale=pos_c4[:, ds(n, 1)]).then_inc(half_ready, 1)
                    if j == 2:
                        wait(act, drive_ready, n)
                        act.wait_ge(half_ready, n + 1)
                        act.activation(root[:, 0:XE], half_tanh[:, 0:XE], ACT.Sqrt, scale=0.25).then_inc(root_ready, 1)
                    if j == 3:
                        act.wait_ge(yb_ready, n + 1)
                        act.wait_ge(params_ready, 1)
                        act.activation(ybh[:, ds(n, 1), :].rearrange("p o n -> p (o n)"), gb_tanh[:, :], ACT.Copy).then_inc(yb_hi, 1)
                return tail

            def lru(n, tail):
                r = rounds(n, PER_LRU, Q_LRU)

                def own(j):
                    if j == 4:
                        e = conv_ext
                        act.wait_ge(chunk_done, r * RING + 4)
                        act.wait_ge(conv_hist_in, n + 1)
                        act.activation(e[:, CH:CH + TH], ps[:, 0, 0:TH], ACT.Copy)
                        act.activation(e[:, CH + TH:CH + SEQ], ps[:, 1, 0:SEQ - TH], ACT.Copy)
                        act.activation(conv_seg(e, CH, NEW), sample_cols(ps[:, 1, SEQ - TH:TH]), ACT.Copy)\
                            .then_inc(conv_ext_ready, 1)
                    if j == 5:
                        act.wait_ge(tap_done[TAPS - 1], n + 1)
                        wait(act, lru_done, n)
                        act.activation(conv_x_hi[:, 0:XE], conv_x[:, 0:XE], ACT.Copy).then_inc(conv_hi, 1)
                    if j == 6:
                        act.wait_ge(small_landed, n * 32 + 32)
                        wait(act, lru_done, n)
                        act.activation(small_hi[:], small_raw[:], ACT.Copy).then_inc(small_hi_ready, 1)
                steps(r, PER_LRU, tail, own)

            lru(0, lambda j: None)
            with act.Fori(1, BLOCKS) as n:
                lru(n, lru_tail(n - 1, rounds(n, PER_LRU, Q_LRU)))

            def merge_round(m):
                act.wait_ge(merge_ready, m + 1)
                act.wait_ge(params_ready, 1)
                act.activation(xh[:, ds(m, 1), :].rearrange("p o n -> p (o n)"), merged[:, :], ACT.Copy, scale=0.5).then_inc(merged_hi, 1)

            def merge_tail(i):
                return lambda j: merge_round(i * 2 + 1) if j == 1 else None

            def proj_b(i, tail, merge_at=5):
                steps(rounds(i, PER_PROJB, Q_PROJB), PER_PROJB, tail, lambda j: merge_round(i * 2) if j == merge_at else None)

            proj_b(0, lru_tail(BLOCKS - 1, Q_PROJB // RING), PER_PROJB - 1)
            act.wait_ge(rows_turned, 1)
            for b in range(3):
                act.activation(rows_sb[:, b], ps[:, 4 + b], ACT.Copy).then_inc(rows_ready, 1)
            with act.Fori(1, DT // 2) as i:
                proj_b(i, merge_tail(i - 1))

            def out_copy(i, m, r, j):
                act.wait_ge(chunk_done, r * RING + j)
                wait(act, out_turned, i * 2 + (m - 1))
                act.activation(halves(out_sb[m][:, :]), pair(m), ACT.Copy).then_inc(out_copied, 1)

            def out_tail(i, r):
                return lambda j: out_copy(i, 1, r, 0) if j == 0 else None

            def project(i, tail, last=False):
                r = rounds(i, PER_OUT, Q_OUT)
                steps(r, PER_OUT, tail, lambda j: out_copy(i, 0, r, 4) if j == 4 else None, last)

            project(0, merge_tail(DT // 2 - 1))
            with act.Fori(1, DT // 2 - 1) as i:
                project(i, out_tail(i - 1, rounds(i, PER_OUT, Q_OUT)))
            project(DT // 2 - 1, out_tail(DT // 2 - 2, rounds(DT // 2 - 1, PER_OUT, Q_OUT)), last=True)
            out_copy(DT // 2 - 1, 1, Q_END // RING, 0)

            act.wait_ge(norm_step, 2)
            act.activation(rstd[1][:, :], rstd[0][:, :], ACT.Sqrt).then_inc(root_var, 1)
            act.wait_ge(shift_ready, 1)
            for t in POOL_TILES:
                act.activation(z[:, t], z[:, t], ACT.Identity, bias=rstd[3][:, t:t + 1], scale=rstd[2][:, t:t + 1])\
                    .then_inc(centred, 1)
            for n, t in enumerate(POOL_TILES):
                act.wait_ge(pool_normed, n + 1)
                store(act, t)

        @block.vector
        def _(dve):
            def split(r, j):
                dve.wait_ge(weight_hi_ready, r * RING + (j + 1))
                dve.tensor_tensor(weight_lo[:, j % RING], weight_raw[:, j % RING], f32(weight_hi[:, j % RING]),
                                  ALU.subtract).then_inc(weight_lo_ready, 1)

            def steps(r, per, tail, own, last=False):
                for j in range(per):
                    if not (last and j + 3 >= per):
                        split(r, j + 3)
                    tail(j)
                    own(j)

            def rest_x(s):
                c, t, n = x_step(s)
                cols = slice(t * P, t * P + n)
                dve.wait_ge(setup_hi, s + 1)
                dve.tensor_tensor(xl[:, CK * c:CK * c + CK, cols], setup_bank(s)[:, 0:CK * n].rearrange("p (k n) -> p k n", n=n),
                                  f32(xh[:, CK * c:CK * c + CK, cols]), ALU.subtract).then_inc(setup_taken, 1)

            setup_order(rest_x, lambda q: split(0, q), SPLIT_BEFORE)
            dve.wait_ge(setup_turned, X_BANKS + 1)
            src = setup_bank(X_BANKS)
            dve.tensor_copy(chan[:, :], src[:, 0:P])
            dve.tensor_scalar(bias_m[:, :], src[:, P:P + 2 * DT + PT_], 0.5, None, ALU.mult).then_inc(setup_taken, 1)
            count = 0

            def param(ins):
                nonlocal count
                count += 1
                ins.then_inc(param_step, 1)
                dve.wait_ge(param_step, count)

            dve.wait_ge(setup_taken, X_BANKS + 1)
            L, (absL, t_exp, u, u2, w) = chan[:, LRU_L:LRU_L + DT], [x[:, :] for x in sp]
            param(dve.scalar_tensor_tensor(out=absL, in0=L, scalar=-1.0, in1=L, op0=ALU.mult, op1=ALU.max))
            param(dve.tensor_scalar(bias_ri[:, :], chan[:, LRU_BA:LRU_BA + 2 * DT], 0.5, None, ALU.mult))
            dve.wait_ge(param_exp, 1)
            param(dve.tensor_scalar(w, t_exp, 2.0, None, ALU.add))
            param(dve.reciprocal(u2, w))
            param(dve.tensor_tensor(u, t_exp, u2, ALU.mult))
            param(dve.tensor_tensor(u2, u, u, ALU.mult))
            param(dve.tensor_scalar(w, u2, 1.0 / 15, None, ALU.mult))
            for k in (13, 11, 9, 7, 5, 3):
                param(dve.scalar_tensor_tensor(out=w, in0=w, scalar=1.0 / k, in1=u2, op0=ALU.add, op1=ALU.mult))
            param(dve.scalar_tensor_tensor(out=w, in0=w, scalar=1.0, in1=u, op0=ALU.add, op1=ALU.mult))
            param(dve.tensor_scalar(u, L, -1.0, 0.0, ALU.mult, ALU.max))
            param(dve.scalar_tensor_tensor(out=w, in0=w, scalar=2.0, in1=u, op0=ALU.mult, op1=ALU.add))
            param(dve.tensor_scalar(neg_c2[:, :], w, -4.0, None, ALU.mult))
            dve.tensor_scalar(pos_c4[:, :], w, 2.0, None, ALU.mult).then_inc(params_ready, 1)
            for j in range(RING - 1):
                split(0, PER_GATE + j)
            for k, (dst, n) in enumerate(((conv_hist[:, :, :], DT * NSEQ * CH), (h_init[:, :, :], DT * NSEQ),
                                          (pool_hist[:, 0:4, :], 4 * NSEQ * HIST), (pool_hist[:, 4:8, :], 4 * NSEQ * HIST))):
                dve.wait_ge(setup_turned, X_BANKS + 2 + k)
                dve.tensor_copy(dst.rearrange("p n s -> p (n s)"), setup_bank(X_BANKS + 1 + k)[:, 0:n]).then_inc(setup_taken, 1)

            none = lambda j: None
            with dve.Fori(1, DT // 2) as i:
                steps(rounds(i, PER_GATE, Q_GATE), PER_GATE, none, none)

            stepped = 0

            def window_op(ins):
                nonlocal stepped
                stepped += 1
                ins.then_inc(window_step, 1)
                dve.wait_ge(window_step, stepped)

            def pool_diff(g, u):
                e, W = pool_ext[u], WIDTHS[g]
                dve.wait_ge(ext_ready, g * 2 + u + 1)
                dve.wait_ge(pads_zero, 2)
                src, w = e, 1
                while w < W:
                    dst = window[0] if src is not window[0] else window[1]
                    window_op(dve.tensor_tensor(dst[:, 2 * w - 1:PEXT], src[:, 2 * w - 1:PEXT], src[:, w - 1:PEXT - w], ALU.add))
                    src, w = dst, 2 * w
                spare = window[0] if src is window[1] else window[1]
                window_op(dve.tensor_tensor(spare[:, 0:W - 1], src[:, HIST:HIST + W - 1], counts[:, 0:W - 1], ALU.mult))
                dve.tensor_tensor(diff[:, 0:W - 1], spare[:, 0:W - 1], e[:, HIST:HIST + W - 1], ALU.subtract)
                dve.scalar_tensor_tensor(out=diff[:, W - 1:SEQ], in0=src[:, HIST + W - 1:HIST + SEQ], scalar=1.0 / W,
                                         in1=e[:, HIST + W - 1:HIST + SEQ], op0=ALU.mult, op1=ALU.subtract)
                dve.scalar_tensor_tensor(out=sample_cols(diff[:, SEQ:T]), in0=pool_seg(src, HIST, NEW), scalar=1.0 / W,
                                         in1=pool_seg(e, HIST, NEW), op0=ALU.mult, op1=ALU.subtract).then_inc(diff_ready, 1)

            def diff_rest(g, u):
                dve.wait_ge(diff_hi, g * 2 + u + 1)
                dve.tensor_tensor(dfl[:, u], diff[:, :], f32(dfh[:, u]), ALU.subtract).then_inc(diff_lo, 1)

            def pool_silu_of(g, u):
                dve.wait_ge(pool_tanh_ready, g * 2 + u + 1)
                dve.scalar_tensor_tensor(out=halves(pool_silu[u][:, :]), in0=halves(pool_tanh[:, :]), scalar=1.0,
                                         in1=pair(2 + u), op0=ALU.add, op1=ALU.mult).then_inc(pool_silu_ready, 1)

            def ya(g, u):
                dve.wait_ge(mixed_done, g * 2 + u + 1)
                dve.wait_ge(pool_silu_ready, g * 2 + u + 1)
                dve.wait_ge(ya_hi, g * 2 + u) if g * 2 + u else None
                dve.scalar_tensor_tensor(out=halves(y_a[:, :]), in0=pair(u), scalar=bias_m[:, 2 * DT + 2 * g + u:2 * DT + 2 * g + u + 1],
                                         in1=halves(pool_silu[u][:, :]), op0=ALU.mult, op1=ALU.mult).then_inc(ya_ready, 1)

            def ya_rest(g, u):
                dve.wait_ge(ya_hi, g * 2 + u + 1)
                dve.tensor_tensor(yal[:, 2 * g + u], y_a[:, :], f32(yah[:, 2 * g + u]), ALU.subtract).then_inc(ya_lo, 1)

            def pool_tail(g):
                def tail(j):
                    if j == 0:
                        pool_silu_of(g, 1)
                    if j == 1:
                        ya(g, 1)
                    if j == 2:
                        ya_rest(g, 1)
                return tail

            def pool_group(g, tail):
                def own(j):
                    if j == 4:
                        pool_diff(g, 0)
                    if j == 6:
                        diff_rest(g, 0)
                    if j == 7:
                        dve.wait_ge(pw_hi_ready, g + 1)
                        dve.tensor_tensor(pw_lo[:], pw_raw[:], f32(pw_hi[:]), ALU.subtract).then_inc(pw_lo_ready, 1)
                    if j == 8:
                        pool_diff(g, 1)
                    if j == 10:
                        diff_rest(g, 1)
                    if j == 12:
                        pool_silu_of(g, 0)
                    if j == 13:
                        ya(g, 0)
                    if j == 14:
                        ya_rest(g, 0)
                steps(rounds(g, PER_POOL, Q_POOL), PER_POOL, tail, own)

            for g in range(GROUPS):
                pool_group(g, pool_tail(g - 1) if g else none)

            def part(i, m, r, j):
                dve.wait_ge(chunk_done, r * RING + j)
                dve.wait_ge(ma_tanh_ready, i * 2 + (m + 1))
                wait(dve, part_spilled[m], i * 16)
                dve.scalar_tensor_tensor(out=halves(part_out[m][:, :]), in0=halves(ma_tanh[m][:, :]), scalar=1.0,
                                         in1=pair(2 + m), op0=ALU.add, op1=ALU.mult).then_inc(part_ready, 1)

            def part_tail(i, r):
                return lambda j: part(i, 1, r, 0) if j == 0 else None

            def proj_a(i, tail):
                r = rounds(i, PER_PROJA, Q_PROJA)
                steps(r, PER_PROJA, tail, lambda j: part(i, 0, r, 10) if j == 10 else None)

            proj_a(0, pool_tail(GROUPS - 1))
            with dve.Fori(1, DT // 2) as i:
                proj_a(i, part_tail(i - 1, rounds(i, PER_PROJA, Q_PROJA)))

            def lru_tail(n):
                X = slice(0, XE)

                def tail(j):
                    if j == 0:
                        dve.wait_ge(gb_tanh_ready, n + 1)
                        dve.scalar_tensor_tensor(out=halves(gb_silu[:, :]), in0=halves(gb_tanh[:, :]), scalar=1.0,
                                                 in1=pair(1), op0=ALU.add, op1=ALU.mult).then_inc(gb_silu_ready, 1)
                    if j == 1:
                        dve.wait_ge(i_ready, n + 1)
                        dve.scalar_tensor_tensor(out=i_tanh[:, X], in0=i_tanh[:, X], scalar=1.0, in1=conv_x[:, X],
                                                 op0=ALU.add, op1=ALU.mult).then_inc(ix_ready, 1)
                        dve.wait_ge(exp_ready, n + 1)
                        dve.wait_ge(half_ready, n + 1)
                        dve.scalar_tensor_tensor(out=decay[:, X], in0=decay[:, X], scalar=1.0, in1=half_tanh[:, X],
                                                 op0=ALU.add, op1=ALU.mult).then_inc(fall_ready, 1)
                        dve.wait_ge(fall_ready, n + 1)
                        dve.tensor_scalar(decay[:, X], decay[:, X], -1.0, 1.0, ALU.mult, ALU.add).then_inc(decay_ready, 1)
                    if j == 2:
                        dve.wait_ge(root_ready, n + 1)
                        dve.wait_ge(decay_ready, n + 1)
                        dve.scalar_tensor_tensor(out=root[:, X], in0=decay[:, X], scalar=1.0, in1=root[:, X],
                                                 op0=ALU.add, op1=ALU.mult).then_inc(scale_ready, 1)
                        dve.wait_ge(scale_ready, n + 1)
                        dve.wait_ge(ix_ready, n + 1)
                        dve.tensor_tensor(i_tanh[:, X], root[:, X], i_tanh[:, X], ALU.mult).then_inc(drive_ready, 1)
                        dve.tensor_tensor(start_term[:, :].rearrange("p (b o) -> p b o", o=1), conv_seg(decay, 0, 1),
                                          h_init[:, ds(n, 1), :].rearrange("p o b -> p b o"), ALU.mult).then_inc(start_ready, 1)
                        dve.wait_ge(drive_ready, n + 1)
                        dve.wait_ge(start_ready, n + 1)
                        dve.tensor_tensor(conv_seg(i_tanh, 0, 1), conv_seg(i_tanh, 0, 1),
                                          start_term[:, :].rearrange("p (b o) -> p b o", o=1), ALU.add)
                        dve.memset(conv_seg(decay, 0, 1), 0.0).then_inc(decay_cut, 1)
                    if j == 3:
                        dve.wait_ge(decay_cut, n + 1)
                        dve.tensor_tensor_scan(half_tanh[:, X], decay[:, X], i_tanh[:, X], 0.0, ALU.mult, ALU.add).then_inc(h_ready, 1)
                        dve.wait_ge(h_ready, n + 1)
                        dve.wait_ge(gb_silu_ready, n + 1)
                        dve.scalar_tensor_tensor(out=gb_tanh[:, 0:SEQ], in0=half_tanh[:, 0:SEQ], scalar=0.5, in1=gb_silu[:, 0:SEQ],
                                                 op0=ALU.mult, op1=ALU.mult)
                        dve.scalar_tensor_tensor(out=sample_cols(gb_tanh[:, SEQ:T]), in0=conv_seg(half_tanh, 0, NEW), scalar=0.5,
                                                 in1=sample_cols(gb_silu[:, SEQ:T]), op0=ALU.mult, op1=ALU.mult).then_inc(yb_ready, 1)
                        dve.wait_ge(yb_hi, n + 1)
                        dve.tensor_tensor(ybl[:, ds(n, 1), :].rearrange("p o n -> p (o n)"), gb_tanh[:, :],
                                          f32(ybh[:, ds(n, 1), :].rearrange("p o n -> p (o n)")), ALU.subtract).then_inc(yb_lo, 1)
                return tail

            def lru(n, tail):
                def own(j):
                    if j == 4:
                        dve.wait_ge(conv_ext_ready, n + 1)
                        dve.wait_ge(pads_zero, 3)
                        dve.tensor_scalar(conv_x[:, 0:XE], conv_ext[:, 0:XE], chan[:, ds(n + CONV_W, 1)], chan[:, ds(n + CONV_B, 1)],
                                          ALU.mult, ALU.add).then_inc(tap_done[0], 1)
                        for k in range(1, TAPS):
                            dve.wait_ge(tap_done[k - 1], n + 1)
                            dve.scalar_tensor_tensor(out=conv_x[:, 0:XE], in0=conv_ext[:, k:k + XE], scalar=chan[:, ds(n + (CONV_W + k * DT), 1)],
                                                     in1=conv_x[:, 0:XE], op0=ALU.mult, op1=ALU.add).then_inc(tap_done[k], 1)
                    if j == 6:
                        dve.wait_ge(conv_hi, n + 1)
                        dve.tensor_tensor(conv_x_lo[:, 0:XE], conv_x[:, 0:XE], f32(conv_x_hi[:, 0:XE]), ALU.subtract).then_inc(conv_lo, 1)
                        dve.wait_ge(small_hi_ready, n + 1)
                        dve.tensor_tensor(small_lo[:], small_raw[:], f32(small_hi[:]), ALU.subtract).then_inc(small_lo_ready, 1)
                steps(rounds(n, PER_LRU, Q_LRU), PER_LRU, tail, own)

            lru(0, part_tail(DT // 2 - 1, Q_LRU // RING))
            with dve.Fori(1, BLOCKS) as n:
                lru(n, lru_tail(n - 1))

            def merge(i, m, r, j):
                dve.wait_ge(chunk_done, r * RING + j)
                dve.wait_ge(gate_loaded[m], i * 32 + 32)
                wait(dve, merged_lo, i * 2 + m)
                dve.scalar_tensor_tensor(out=halves(merged[:, :]), in0=halves(gate_in[m][:, :]), scalar=1.0, in1=pair(m),
                                         op0=ALU.add, op1=ALU.mult).then_inc(gated_ready, 1)
                dve.wait_ge(gated_ready, i * 2 + (m + 1))
                dve.tensor_tensor(merged[:, :], merged[:, :], part_in[m][:, :], ALU.add).then_inc(merge_ready, 1)

            def merge_rest(m):
                dve.wait_ge(merged_hi, m + 1)
                dve.scalar_tensor_tensor(out=xl[:, ds(m, 1), :].rearrange("p o n -> p (o n)"), in0=merged[:, :], scalar=0.5,
                                         in1=f32(xh[:, ds(m, 1), :].rearrange("p o n -> p (o n)")),
                                         op0=ALU.mult, op1=ALU.subtract).then_inc(merged_lo, 1)

            def merge_tail(i, r):
                def tail(j):
                    if j == 0:
                        merge(i, 1, r, 0)
                    if j == 1:
                        merge_rest(i * 2 + 1)
                return tail

            def proj_b(i, tail, merge_at=(4, 5)):
                r = rounds(i, PER_PROJB, Q_PROJB)

                def own(j):
                    if j == merge_at[0]:
                        merge(i, 0, r, j)
                    if j == merge_at[1]:
                        merge_rest(i * 2)
                steps(r, PER_PROJB, tail, own)

            proj_b(0, lru_tail(BLOCKS - 1), (PER_PROJB - 1, PER_PROJB - 1))
            with dve.Fori(1, DT // 2) as i:
                proj_b(i, merge_tail(i - 1, rounds(i, PER_PROJB, Q_PROJB)))

            def residual(i, m):
                tile_ = i * 2 + m
                dve.wait_ge(z_loaded, 16 * (XT + 3))
                dve.wait_ge(out_turned, tile_ + 1)
                zp = z[:, 0:XT, ds(tile_ * P, P)]
                dve.scalar_tensor_tensor(out=zp, in0=zp, scalar=ALPHA, in1=ps[:, 4 + 2 * m].rearrange("p (t n) -> p t n", n=P),
                                         op0=ALU.mult, op1=ALU.add)
                zs = z[0:SAMP, XT, ds(tile_ * P, P)]
                dve.scalar_tensor_tensor(out=zs, in0=zs, scalar=ALPHA, in1=ps[0:SAMP, 5 + 2 * m, 0:P],
                                         op0=ALU.mult, op1=ALU.add).then_inc(z_added, 1)

            def statistics(i, m):
                tile_ = i * 2 + m
                dve.wait_ge(z_added, tile_ + 1)
                for t in range(XT + 1):
                    n = P if t < XT else SAMP
                    ins = dve.bn_stats(stats[0:n, t, ds(tile_, 1), :].rearrange("p o s -> p (o s)"), z[0:n, t, ds(tile_ * P, P)])
                ins.then_inc(z_stats, 1)

            def out_tail(i):
                def tail(j):
                    if j == 2:
                        residual(i, 1)
                    if j == 3:
                        statistics(i, 1)
                return tail

            def project(i, tail, last=False):
                def own(j):
                    if j == 6:
                        residual(i, 0)
                    if j == 7:
                        statistics(i, 0)
                steps(rounds(i, PER_OUT, Q_OUT), PER_OUT, tail, own, last)

            project(0, merge_tail(DT // 2 - 1, Q_OUT // RING))
            with dve.Fori(1, DT // 2 - 1) as i:
                project(i, out_tail(i - 1))
            project(DT // 2 - 1, out_tail(DT // 2 - 2), last=True)
            residual(DT // 2 - 1, 1)
            statistics(DT // 2 - 1, 1)

            dve.wait_ge(z_stats, DT)
            dve.memset(moments[:], 1.0).then_inc(norm_step, 1)
            dve.wait_ge(norm_step, 1)
            for t in range(XT + 1):
                n = P if t < XT else SAMP
                ins = dve.bn_aggr(moments[0:n, t, :], stats[0:n, t].rearrange("p m s -> p (m s)"))
            ins.then_inc(moments_ready, 1)
            dve.wait_ge(moments_ready, 1)
            mean, var = moments[:, :, 0], moments[:, :, 1]
            v, y, y2, t3 = (x[:, :] for x in (rstd[0], rstd[2], rstd[1], rstd[3]))
            dve.tensor_scalar(v, var, EPS, None, ALU.add).then_inc(norm_step, 1)
            dve.wait_ge(root_var, 1)
            norm = 2

            def link(ins):
                nonlocal norm
                norm += 1
                ins.then_inc(norm_step, 1)
                dve.wait_ge(norm_step, norm)

            link(dve.reciprocal(y, y2))
            link(dve.tensor_tensor(t3, y, y, ALU.mult))
            link(dve.tensor_tensor(t3, t3, v, ALU.mult))
            link(dve.tensor_scalar(t3, t3, -0.5, 1.5, ALU.mult, ALU.add))
            link(dve.tensor_tensor(y, y, t3, ALU.mult))
            dve.scalar_tensor_tensor(out=t3, in0=mean, scalar=-1.0, in1=y, op0=ALU.mult, op1=ALU.mult).then_inc(shift_ready, 1)
            for k, t in enumerate(DVE_TILES):
                n = P if t < XT else SAMP
                zt = z[0:n, t]
                link(dve.scalar_tensor_tensor(out=zt, in0=zt, scalar=moments[0:n, t, 0:1], in1=gamma[0:n, :],
                                              op0=ALU.subtract, op1=ALU.mult))
                dve.scalar_tensor_tensor(out=zt, in0=zt, scalar=rstd[2][0:n, t:t + 1], in1=beta[0:n, :],
                                         op0=ALU.mult, op1=ALU.add).then_inc(normed, 1)

        @block.tensor
        def _(pe):
            def products(out_halves, hi, lo, xs_h, xs_l, first, last):
                n = 0
                terms = ((hi, xs_h), (hi, xs_l), (lo, xs_h))
                for w, xs in terms:
                    for h in range(2):
                        ins = pe.matmul(out_halves[h], w, xs[h], start=first and n == 0, stop=last and n == 2)
                    n += 1
                return ins

            def chunk(r, j, p, rhs_h, rhs_l, k0, ks):
                pe.wait_ge(weight_lo_ready, r * RING + (j + 1))
                for c in range(CK):
                    k = k0 + c
                    ins = products([ps[:, 2 * p + h, 0:TH] for h in range(2)], weight_hi[:, j % RING, c, :], weight_lo[:, j % RING, c, :],
                                   [rhs_h[:, k, h * TH:(h + 1) * TH] for h in range(2)],
                                   [rhs_l[:, k, h * TH:(h + 1) * TH] for h in range(2)], k == 0, k == ks - 1)
                ins.then_inc(chunk_done, 1)

            def x_tile(r, j, p):
                for c in range(DT // CK):
                    chunk(r, j + c, p, xh, xl, c * CK, DT)

            def bank_of(s):
                wait(pe, setup_taken, s - 3)
                return setup_bank(s)

            def turn_x(s):
                c, t, n = x_step(s)
                pe.wait_ge(x_landed[c], 32)
                b = bank_of(s)
                for k in range(CK):
                    ins = pe.transpose(b[:, k * n:(k + 1) * n], x_rows[0:n, t, (CK * c + k) * P:(CK * c + k + 1) * P], ident[0:n, 0:n])
                ins.then_inc(setup_turned, 1)

            def turn_params():
                pe.wait_ge(consts_landed, 16 * 8)
                b = bank_of(X_BANKS)
                pe.transpose(b[:, 0:P], chan_rows[:, :], ident[:, :])
                nb = 2 * DT + PT_
                pe.transpose(b[:, P:P + nb], bias_rows[:, :], ident[0:nb, 0:nb]).then_inc(setup_turned, 1)

            def first_chunk(q):
                c, m = divmod(q, 2)
                if q == PER_GATE - 1:
                    turn_params()
                if m == 0:
                    pe.wait_ge(setup_taken, (c + 1) * (XT + 1))
                chunk(0, q, m, xh, xl, c * CK, DT)

            pe.wait_ge(ident_landed, 16)
            setup_order(turn_x, first_chunk, TURNED_BEFORE)
            pe.wait_ge(states_landed, 48)
            for s, state, rows, ks in ((1, conv_state, NSEQ * CH, range(DT)), (2, h_state, NSEQ, range(DT)),
                                       (3, pool_state, NSEQ * HIST, range(4)), (4, pool_state, NSEQ * HIST, range(4, 8))):
                b = bank_of(X_BANKS + s)
                for n, k in enumerate(ks):
                    ins = pe.transpose(b[:, n * rows:(n + 1) * rows], state[:, k * P:(k + 1) * P], ident[0:rows, 0:rows])
                ins.then_inc(setup_turned, 1)

            def gate(i):
                for m in range(2):
                    wait(pe, gate_tanh_ready, i * 2 + (m - 1))
                    x_tile(rounds(i, PER_GATE, Q_GATE), 4 * m, m)

            with pe.Fori(1, DT // 2) as i:
                gate(i)

            def pool_group(g):
                r = rounds(g, PER_POOL, Q_POOL)
                for u in range(2):
                    pe.wait_ge(gate_tanh_ready, DT - 1 + u)
                    wait(pe, ya_ready, g * 2 + (u - 1))
                    x_tile(r, 4 * u, u)
                pe.wait_ge(setup_taken, SETUP_BANKS)
                wait(pe, pool_silu_ready, g * 2 - 1)
                x_tile(r, 8, 2)
                pe.wait_ge(pw_lo_ready, g + 1)
                pe.wait_ge(diff_lo, g * 2 + 2)
                for j in range(2):
                    for k in range(2):
                        ins = products([ps[:, 2 * j + h, 0:TH] for h in range(2)], pw_hi[:, k, j * P:(j + 1) * P], pw_lo[:, k, j * P:(j + 1) * P],
                                       [dfh[:, k, h * TH:(h + 1) * TH] for h in range(2)],
                                       [dfl[:, k, h * TH:(h + 1) * TH] for h in range(2)], k == 0, k == 1)
                    ins.then_inc(mixed_done, 1)
                wait(pe, pool_silu_ready, g * 2)
                x_tile(r, 12, 3)

            pool_group(0)
            with pe.Fori(1, GROUPS) as g:
                pool_group(g)

            def proj_a(i):
                r = rounds(i, PER_PROJA, Q_PROJA)
                for m in range(2):
                    pe.wait_ge(ya_ready, PT_ - 1 + m)
                    wait(pe, ma_tanh_ready, i * 2 + (m - 1))
                    x_tile(r, 4 * m, m)
                pe.wait_ge(ya_lo, PT_)
                for m in range(2):
                    wait(pe, part_ready, i * 2 + (m - 1))
                    for c in range(2):
                        chunk(r, 8 + 2 * m + c, 2 + m, yah, yal, c * CK, PT_)

            proj_a(0)
            with pe.Fori(1, DT // 2) as i:
                proj_a(i)

            def lru(n):
                r = rounds(n, PER_LRU, Q_LRU)
                pe.wait_ge(ma_tanh_ready, DT)
                wait(pe, conv_ext_ready, n)
                x_tile(r, 0, 0)
                wait(pe, gb_silu_ready, n)
                x_tile(r, 4, 1)
                pe.wait_ge(part_ready, DT)
                wait(pe, i_ready, n)
                pe.wait_ge(conv_lo, n + 1)
                pe.wait_ge(small_lo_ready, n + 1)
                for k in range(2):
                    ins = products([ps[:, 4 + 2 * k + h, 0:XEH] for h in range(2)], small_hi[:, k, :], small_lo[:, k, :],
                                   [conv_x_hi[:, h * XEH:(h + 1) * XEH] for h in range(2)],
                                   [conv_x_lo[:, h * XEH:(h + 1) * XEH] for h in range(2)], True, True)
                ins.then_inc(lru_done, 1)

            lru(0)
            with pe.Fori(1, BLOCKS) as n:
                lru(n)

            def proj_b(i):
                r = rounds(i, PER_PROJB, Q_PROJB)
                for m in range(2):
                    pe.wait_ge(gb_silu_ready, BLOCKS)
                    wait(pe, merge_ready, i * 2 + (m - 1))
                    for c in range(DT // CK):
                        pe.wait_ge(yb_lo, (c + 1) * CK)
                        chunk(r, 4 * m + c, m, ybh, ybl, c * CK, DT)

            for j, (m, c) in enumerate(PROJB_FIRST):
                pe.wait_ge(gb_silu_ready if m else conv_ext_ready, BLOCKS)
                pe.wait_ge(yb_lo, (c + 1) * CK)
                chunk(Q_PROJB // RING, j, m, ybh, ybl, c * CK, DT)
            pe.wait_ge(h_kept, BLOCKS)
            flat = lambda t: t[:, :, :].rearrange("p s j -> p (s j)")
            tiles = [(0, flat(pool_rows), HIST * PT_ + c * P, c) for c in range(4)]
            tiles += [(1, flat(pool_rows), 0, 0), (1, flat(h_rows), 0, 1), (1, flat(h_rows), DT, 2)]
            tiles += [(2, flat(conv_rows), CH * DT + c * P, c) for c in range(3)] + [(2, flat(conv_rows), 0, 3)]
            for b, src, first, c in tiles:
                ins = pe.transpose(ps[:, 4 + b, c * P:(c + 1) * P], src[:, first:first + P], ident[:, :])
            ins.then_inc(rows_turned, 1)
            with pe.Fori(1, DT // 2) as i:
                proj_b(i)

            def turn(i, m):
                pe.wait_ge(out_copied, i * 2 + (m + 1))
                pe.wait_ge(rows_ready, 3)
                wait(pe, z_added, i * 2 + (m - 1))
                for t in range(XT):
                    pe.transpose(ps[:, 4 + 2 * m, t * P:(t + 1) * P], out_sb[m][:, t * P:(t + 1) * P], ident[:, :])
                pe.transpose(ps[0:SAMP, 5 + 2 * m, 0:P], out_sb[m][:, SEQ:T], ident[:, :]).then_inc(out_turned, 1)

            def project(i, before):
                r = rounds(i, PER_OUT, Q_OUT)
                for m in range(2):
                    pe.wait_ge(merge_ready, DT - 1 + m)
                    wait(pe, out_copied, i * 2 + (m - 1))
                    for c in range(DT // CK):
                        pe.wait_ge(merged_lo, (c + 1) * CK)
                        chunk(r, 4 * m + c, m, xh, xl, c * CK, DT)
                        if c == 0 and (m or before is not None):
                            turn(*((i, 0) if m else (before, 1)))

            project(0, None)
            with pe.Fori(1, DT // 2) as i:
                project(i, i - 1)
            turn(DT // 2 - 1, 1)


def kernel(**inputs):
    import numpy as np
    import concourse.bacc as bacc
    from concourse.bass_utils import run_bass_kernel_spmd

    nc = bacc.Bacc("TRN2", target_bir_lowering=False, num_devices=1)
    arrays = {f"in_{n}": np.ascontiguousarray(inputs[n]) for n in INPUTS}
    hist = inputs["state_pool"].shape[2]
    arrays["identity"] = np.eye(P, dtype=np.float32)
    arrays["reciprocals"] = np.broadcast_to((1.0 / np.arange(1, hist + 1)).astype(np.float32), (P, hist)).copy()
    aps = {n: nc.dram_tensor(n, v.shape, mybir.dt.from_np(v.dtype), kind="ExternalInput").ap() for n, v in arrays.items()}
    names = ("x_prompt", "x_sample", "state_pool", "state_conv", "state_h")
    prompt, sample, spool, sconv, sh = (inputs[n].shape for n in names)
    shapes = [prompt, sample,
              (spool[0], prompt[0], *spool[2:]), (sconv[0], prompt[0], *sconv[2:]), (sh[0], prompt[0], sh[2]),
              spool, sconv, sh]
    outs = [nc.dram_tensor(f"out_{i}", s, F32, kind="ExternalOutput").ap() for i, s in enumerate(shapes)]
    build(nc, {n: aps[f"in_{n}"] for n in INPUTS}, aps, outs)
    r = run_bass_kernel_spmd(nc, [arrays], core_ids=[0])
    return tuple(r.results[0][f"out_{i}"] for i in range(len(outs)))
```

```python
from contextlib import ExitStack

import concourse.bass as bass
from concourse import mybir

P = 128
F32 = mybir.dt.float32
F32R = mybir.dt.float32r
ALU = mybir.AluOpType
ACT = mybir.ActivationFunctionType
ds = bass.ds

INPUTS = ["x_prompt", "x_sample", "state_pool", "state_conv", "state_h", "w_in", "b_merge", "pool_w",
          "pool_scale", "conv_w", "conv_b", "lru_wa", "lru_ba", "lru_wx", "lru_bx", "lru_L",
          "w_proj_a", "w_proj_b", "w_out", "ln_g", "ln_b"]


def build(nc, a, host, out):
    SEQ, D = a["x_prompt"].shape[1:]
    NSEQ, NEW = a["x_sample"].shape[:2]
    HIST, PW = a["state_pool"].shape[2:]
    CH = a["state_conv"].shape[2]
    TAPS = CH + 1
    GROUPS = a["pool_w"].shape[1]
    GD = PW // GROUPS
    SAMP = NSEQ * NEW
    T = SEQ + SAMP
    TH = T // 2
    DT, PT_ = D // P, PW // P
    BLOCKS = a["lru_wa"].shape[1]
    CK = 4
    RING = 4
    WIDTHS = (2, 4, 8, 16)
    ALPHA = 2.0 ** 0.25
    EPS = 1e-5
    XT = SEQ // P
    PSEG, CSEG = HIST + NEW, CH + NEW
    PEXT = HIST + SEQ + NSEQ * PSEG
    CEXT = CH + SEQ + NSEQ * CSEG
    XE = CEXT - CH
    XEH = XE // 2
    SROWS = 1 + NSEQ
    PROWS, CROWS = HIST + SAMP, CH * SROWS

    COL_UA, COL_GA, COL_UB = 0, PW, 2 * PW
    COL_GB, COL_MA = COL_UB + D, COL_UB + 2 * D
    COL_MB = COL_MA + D
    PER_GATE, PER_POOL, PER_PROJA, PER_LRU, PER_PROJB, PER_OUT = 8, 16, 12, 8, 8, 8
    Q_GATE = 0
    Q_POOL = Q_GATE + DT // 2 * PER_GATE
    Q_PROJA = Q_POOL + GROUPS * PER_POOL
    Q_LRU = Q_PROJA + DT // 2 * PER_PROJA
    Q_PROJB = Q_LRU + BLOCKS * PER_LRU
    Q_OUT = Q_PROJB + DT // 2 * PER_PROJB
    Q_END = Q_OUT + DT // 2 * PER_OUT

    x_prompt = a["x_prompt"][0].rearrange("(t p) d -> t p d", p=P)
    x_sample = a["x_sample"].rearrange("b s d -> (b s) d")
    y_prompt = out[0][0].rearrange("(t p) d -> t p d", p=P)
    y_sample = out[1].rearrange("b s d -> (b s) d")
    w_in, w_pa, w_pb, w_out = a["w_in"][0], a["w_proj_a"][0], a["w_proj_b"][0], a["w_out"][0]
    gate_b_dram = nc.dram_tensor("gate_b_scratch", (DT, P, T), F32, kind="Internal").ap()
    part_a_dram = nc.dram_tensor("part_a_scratch", (DT, P, T), F32, kind="Internal").ap()
    EARLY, LATE = range(0, XT // 2), range(XT // 2, XT + 1)
    TE = len(EARLY) * P
    TL = T - TE
    POOL_PARTS = ((P, LATE[-2], slice(D // 2, D)), (SAMP, XT, slice(0, D)))
    SHIFT_ROWS = 66
    ROW_STORES = NSEQ + 7
    STORES = 1 + len(LATE) + 1 + 2 * len(EARLY)
    XBLOCKS = DT // CK
    X_BANKS = XBLOCKS * (XT + 1)
    SETUP_BANKS = X_BANKS + 5

    with ExitStack() as ctx:
        def sem(name):
            return ctx.enter_context(nc.semaphore(name))

        def alloc(stack, name, shape, dt=F32):
            return stack.enter_context(nc.sbuf_tensor(name, shape, dt))

        xh = alloc(ctx, "xh", [P, DT, T], F32R)
        xl = alloc(ctx, "xl", [P, DT, T], F32R)
        weight_raw = alloc(ctx, "weight_raw", [P, RING, CK, P])
        weight_hi = alloc(ctx, "weight_hi", [P, RING, CK, P], F32R)
        weight_lo = alloc(ctx, "weight_lo", [P, RING, CK, P], F32R)
        ident = alloc(ctx, "ident", [P, P])
        counts = alloc(ctx, "counts", [P, HIST])
        chan = alloc(ctx, "chan", [P, 8 * DT])
        bias_m = alloc(ctx, "bias_m", [P, 2 * DT + PT_])
        bias_ri = alloc(ctx, "bias_ri", [P, 2 * DT])
        neg_c2 = alloc(ctx, "neg_c2", [P, DT])
        pos_c4 = alloc(ctx, "pos_c4", [P, DT])
        conv_hist = alloc(ctx, "conv_hist", [P, DT, NSEQ * CH])
        h_init = alloc(ctx, "h_init", [P, DT, NSEQ])
        pool_rows = alloc(ctx, "pool_rows", [P, PROWS, PT_])
        conv_rows = alloc(ctx, "conv_rows", [P, CROWS, DT])
        h_rows = alloc(ctx, "h_rows", [P, SROWS, DT])
        start_term = alloc(ctx, "start_term", [P, NSEQ])
        CONV_W, CONV_B, LRU_BA, LRU_BX, LRU_L = 0, TAPS * DT, (TAPS + 1) * DT, (TAPS + 2) * DT, (TAPS + 3) * DT

        with ExitStack() as s:
            x_rows = alloc(s, "x_rows", [P, XT + 1, D])
            conv_state = alloc(s, "conv_state", [NSEQ * CH, D])
            h_state = alloc(s, "h_state", [NSEQ, D])
            pool_state = alloc(s, "pool_state", [NSEQ * HIST, PW])
            chan_rows = alloc(s, "chan_rows", [P, P])
            bias_rows = alloc(s, "bias_rows", [2 * DT + PT_, P])
            sp = [alloc(s, f"softplus{i}", [P, DT]) for i in range(5)]
        with ExitStack() as s:
            yah = alloc(s, "yah", [P, PT_, T], F32R)
            yal = alloc(s, "yal", [P, PT_, T], F32R)
            pool_ext = [alloc(s, f"pool_ext{i}", [P, PEXT]) for i in range(2)]
            window = [alloc(s, f"window{i}", [P, PEXT]) for i in range(2)]
            diff = alloc(s, "diff", [P, T])
            dfh = alloc(s, "dfh", [P, 2, T], F32R)
            dfl = alloc(s, "dfl", [P, 2, T], F32R)
            pool_tanh = alloc(s, "pool_tanh", [P, T])
            pool_silu = [alloc(s, f"pool_silu{i}", [P, T]) for i in range(2)]
            y_a = alloc(s, "y_a", [P, T])
        with ExitStack() as s:
            ybh = alloc(s, "ybh", [P, DT, T], F32R)
            ybl = alloc(s, "ybl", [P, DT, T], F32R)
        with ExitStack() as s:
            z = alloc(s, "z", [P, XT + 1, D])
            gamma = alloc(s, "gamma", [P, D])
            beta = alloc(s, "beta", [P, D])
            out_sb = [alloc(s, f"out_sb{i}", [P, T]) for i in range(2)]
            minus_one = alloc(s, "minus_one", [P, 4])
            stats = alloc(s, "stats", [P, XT + 1, DT, 6])
            moments = alloc(s, "moments", [P, XT + 1, 2])
            rstd = [alloc(s, f"rstd{i}", [P, XT + 1]) for i in range(4)]
            scale_raw = alloc(s, "scale_raw", [P, D])
        big = ctx.enter_context(nc.sbuf_tensor("big_region", [P, 2 * DT * T], F32))
        with ExitStack() as s:
            conv_x_hi = alloc(s, "conv_x_hi", [P, CEXT], F32R)
            conv_x_lo = alloc(s, "conv_x_lo", [P, CEXT], F32R)
            conv_ext = alloc(s, "conv_ext", [P, CEXT])
            r_tanh = alloc(s, "r_tanh", [P, CEXT])
            small_raw = alloc(s, "small_raw", [P, 2, P])
            small_hi = alloc(s, "small_hi", [P, 2, P], F32R)
            small_lo = alloc(s, "small_lo", [P, 2, P], F32R)
            i_tanh = alloc(s, "i_tanh", [P, CEXT])
            decay = alloc(s, "decay", [P, CEXT])
            half_tanh = alloc(s, "half_tanh", [P, CEXT])
            root = alloc(s, "root", [P, CEXT])
            conv_x = alloc(s, "conv_x", [P, CEXT])
            gb_tanh = alloc(s, "gb_tanh", [P, T])
            gb_silu = alloc(s, "gb_silu", [P, T])
        with ExitStack() as s:
            gate_out = [alloc(s, f"gate_out{i}", [P, T]) for i in range(2)]
            ma_tanh = [alloc(s, f"ma_tanh{i}", [P, T]) for i in range(2)]
            part_out = [alloc(s, f"part_out{i}", [P, T]) for i in range(2)]
            pool_hist = alloc(s, "pool_hist", [P, PT_, NSEQ * HIST])
            pw_raw = alloc(s, "pw_raw", [P, 2, GD])
            pw_hi = alloc(s, "pw_hi", [P, 2, GD], F32R)
            pw_lo = alloc(s, "pw_lo", [P, 2, GD], F32R)
        with ExitStack() as s:
            gate_in = [alloc(s, f"gate_in{i}", [P, T]) for i in range(2)]
            part_in = [alloc(s, f"part_in{i}", [P, T]) for i in range(2)]
            alloc(s, "below_merged", [P, 876])
            merged = alloc(s, "merged", [P, T])
            rows_sb = alloc(s, "rows_sb", [P, 3, 4 * P])
        with ExitStack() as s:
            more_lo = alloc(s, "more_lo", [P, RING, CK, P], F32R)
            shift_cols = alloc(s, "shift_cols", [P, len(EARLY), SHIFT_ROWS])
            shift_rows = alloc(s, "shift_rows", [P, len(EARLY), P], F32R)
            alloc(s, "below_more_hi", [P, (4 * T + 876 + T) - RING * CK * P - len(EARLY) * (SHIFT_ROWS + P)])
            more_hi = alloc(s, "more_hi", [P, RING, CK, P], F32R)
            scale_rows = alloc(s, "scale_rows", [P, D], F32R)
        with ExitStack() as s:
            bracket = alloc(s, "bracket", [P, D // 2])
        ps = ctx.enter_context(nc.psum_tensor("ps", [P, 8, 512], F32))

        def pair(i, n=TH):
            return ps[:, 2 * i:2 * i + 2, 0:n]

        def halves(ap):
            return ap.rearrange("p (h n) -> p h n", h=2)

        def f32(ap):
            return ap.bitcast(F32)

        def conv_seg(buf, off, n):
            v = buf[:, CH + SEQ:CH + SEQ + NSEQ * CSEG].rearrange("p (b s) -> p b s", s=CSEG)
            return v[:, :, off:off + n]

        def pool_seg(buf, off, n):
            v = buf[:, HIST + SEQ:HIST + SEQ + NSEQ * PSEG].rearrange("p (b s) -> p b s", s=PSEG)
            return v[:, :, off:off + n]

        def sample_cols(ap):
            return ap.rearrange("p (b s) -> p b s", s=NEW)

        def gate_col(which, m):
            return bias_m[:, ds(which * DT + m, 1)]

        raw_landed = [sem(f"raw_landed{i}") for i in range(RING)]
        weight_hi_ready, weight_lo_ready, chunk_done = sem("weight_hi_ready"), sem("weight_lo_ready"), sem("chunk_done")
        x_landed = [sem(f"x_landed{i}") for i in range(XBLOCKS)]
        ident_landed, consts_landed, states_landed = sem("ident_landed"), sem("consts_landed"), sem("states_landed")
        setup_turned, setup_hi, setup_taken = sem("setup_turned"), sem("setup_hi"), sem("setup_taken")
        param_step, param_exp, params_ready = sem("param_step"), sem("param_exp"), sem("params_ready")
        pads_zero = sem("pads_zero")
        gate_tanh_ready = sem("gate_tanh_ready")
        gate_spilled = [sem(f"gate_spilled{i}") for i in range(2)]
        hist_in, ext_ready, rows_kept = sem("pool_hist_in"), sem("pool_ext_ready"), sem("pool_rows_kept")
        window_step, diff_ready, diff_hi, diff_lo = sem("window_step"), sem("diff_ready"), sem("diff_hi"), sem("diff_lo")
        pw_landed, pw_hi_ready, pw_lo_ready, mixed_done = sem("pw_landed"), sem("pw_hi_ready"), sem("pw_lo_ready"), sem("mixed_done")
        pool_tanh_ready, pool_silu_ready, ya_ready, ya_hi, ya_lo = (
            sem("pool_tanh_ready"), sem("pool_silu_ready"), sem("ya_ready"), sem("ya_hi"), sem("ya_lo"))
        ma_tanh_ready, part_ready = sem("ma_tanh_ready"), sem("part_ready")
        part_spilled = [sem(f"part_spilled{i}") for i in range(2)]
        conv_hist_in, conv_ext_ready, conv_rows_kept = sem("conv_hist_in"), sem("conv_ext_ready"), sem("conv_rows_kept")
        tap_done = [sem(f"tap_done{i}") for i in range(TAPS)]
        conv_hi, conv_lo = sem("conv_hi"), sem("conv_lo")
        small_landed, small_hi_ready, small_lo_ready, lru_done = (
            sem("small_landed"), sem("small_hi_ready"), sem("small_lo_ready"), sem("lru_done"))
        gb_tanh_ready, gb_silu_ready, r_ready, i_ready = sem("gb_tanh_ready"), sem("gb_silu_ready"), sem("r_ready"), sem("i_ready")
        exp_ready, half_ready, root_ready = sem("exp_ready"), sem("half_ready"), sem("root_ready")
        ix_ready, fall_ready, decay_ready, scale_ready, drive_ready = (
            sem("ix_ready"), sem("fall_ready"), sem("decay_ready"), sem("scale_ready"), sem("drive_ready"))
        start_ready, decay_cut, h_ready, h_kept = sem("start_ready"), sem("decay_cut"), sem("h_ready"), sem("h_kept")
        yb_ready, yb_hi, yb_lo = sem("yb_ready"), sem("yb_hi"), sem("yb_lo")
        gate_loaded = [sem(f"gate_loaded{i}") for i in range(2)]
        gated_ready, merge_ready, merged_hi, merged_lo = sem("gated_ready"), sem("merge_ready"), sem("merged_hi"), sem("merged_lo")
        rows_turned, rows_ready = sem("rows_turned"), sem("rows_ready")
        z_loaded, moments_ready, shift_ready = sem("z_loaded"), sem("moments_ready"), sem("shift_ready")
        early_done, z_scaled, var_ready, y_ready = sem("early_done"), sem("z_scaled"), sem("var_ready"), sem("y_ready")
        preset, bracket_ready = sem("preset"), sem("bracket_ready")
        rows_zero, scale_loaded, scale_hi, scale_lo = sem("rows_zero"), sem("scale_loaded"), sem("scale_hi"), sem("scale_lo")
        shift_turned, shift_hi, shift_lo, shift_spread = sem("shift_turned"), sem("shift_hi"), sem("shift_lo"), sem("shift_spread")
        pool_scaled, pool_normed = sem("pool_scaled"), sem("pool_normed")
        out_copied, out_turned, z_added, z_stats = sem("out_copied"), sem("out_turned"), sem("z_added"), sem("z_stats")
        norm_step, root_var, centred, normed = sem("norm_step"), sem("root_var"), sem("centred"), sem("normed")
        stored, rows_stored = sem("stored"), sem("rows_stored")

        block = ctx.enter_context(nc.Block())

        def wait(eng, s, value):
            if isinstance(value, int) and value <= 0:
                return
            eng.wait_ge(s, value)

        def rounds(i, per, q0):
            return i * (per // RING) + q0 // RING

        def setup_bank(s):
            return ps[:, 4 + s % 4]

        def x_step(s):
            c, t = divmod(s, XT + 1)
            return c, t, P if t < XT else SAMP

        TURNED_BEFORE = [9, 13, 17] + [X_BANKS] * (PER_GATE - 3)
        SPLIT_BEFORE = [5, 9, 13, 17] + [X_BANKS] * (PER_GATE - 4)

        def setup_order(x_bank, chunk, before):
            done = 0
            for q in range(PER_GATE):
                for s in range(done, before[q]):
                    x_bank(s)
                done = before[q]
                chunk(q)

        PROJB_FIRST = [(m, c) for m in range(2) for c in range(DT // CK - 1)] + [(m, DT // CK - 1) for m in range(2)]

        @block.sync
        def _(sync):
            def tile(w, m, r, j, base=0, rows=D, paired=0):
                w = w[:, base:base + min(w.shape[1] - base, D)].rearrange("k (m n) -> k m n", n=P)
                for k in range(j, j + rows // (CK * P)):
                    if paired and k % 2 and k + 1 < paired:
                        wait(sync, weight_lo_ready, r * RING + (k + 2 - RING))
                    elif not paired or k % 2 or k == 0:
                        wait(sync, weight_lo_ready, r * RING + (k + 1 - RING))
                    sync.dma_start(weight_raw[:, k % RING],
                                   w[(k - j) * CK * P:(k - j + 1) * CK * P, ds(m, 1), :].rearrange("(c p) o n -> p c (o n)", p=P))\
                        .then_inc(raw_landed[k % RING], 16)

            def load_x(c):
                cols = slice(c * CK * P, (c + 1) * CK * P)
                sync.dma_start(x_rows[:, 0:XT, cols], a["x_prompt"][0][:, cols].rearrange("(t p) d -> p t d", p=P)).then_inc(x_landed[c], 16)
                sync.dma_start(x_rows[0:SAMP, XT, cols], x_sample[:, cols]).then_inc(x_landed[c], 16)

            def load_chunk(q):
                c, m = divmod(q, 2)
                wait(sync, weight_lo_ready, q + 1 - RING)
                sync.dma_start(weight_raw[:, q % RING],
                               w_in[c * CK * P:(c + 1) * CK * P, COL_MB + m * P:COL_MB + (m + 1) * P].rearrange("(c p) n -> p c n", p=P))\
                    .then_inc(raw_landed[q % RING], 16)

            def gate(i):
                for m in range(2):
                    tile(w_in, i * 2 + m, rounds(i, PER_GATE, Q_GATE), 4 * m, COL_MB)

            load_x(0)
            for q in range(PER_GATE):
                load_chunk(q)
                if q in (0, 1, 3):
                    load_x(q // 2 + 1 + q % 2)
            sync.dma_start(conv_state[:, :], a["state_conv"][0].rearrange("b s d -> (b s) d")).then_inc(states_landed, 16)
            sync.dma_start(h_state[:, :], a["state_h"][0]).then_inc(states_landed, 16)
            sync.dma_start(pool_state[:, :], a["state_pool"][0].rearrange("b s d -> (b s) d")).then_inc(states_landed, 16)
            sync.dma_start(out[5][0][:, 0:HIST - NEW, :], a["state_pool"][0][:, NEW:, :]).then_inc(stored, 16)
            with sync.Fori(1, DT // 2) as i:
                gate(i)
            with sync.Fori(0, GROUPS) as g:
                for n, part in enumerate((COL_UA, COL_UA + P, COL_GA, COL_GA + P)):
                    tile(w_in, g * (GD // P), rounds(g, PER_POOL, Q_POOL), 4 * n, part)
            with sync.Fori(0, DT // 2) as i:
                for m in range(2):
                    tile(w_in, i * 2 + m, rounds(i, PER_PROJA, Q_PROJA), 4 * m, COL_MA, paired=PER_PROJA)
                for m in range(2):
                    tile(w_pa, i * 2 + m, rounds(i, PER_PROJA, Q_PROJA), 8 + 2 * m, rows=PW, paired=PER_PROJA)
            with sync.Fori(0, BLOCKS) as n:
                tile(w_in, n, rounds(n, PER_LRU, Q_LRU), 0, COL_UB)
                tile(w_in, n, rounds(n, PER_LRU, Q_LRU), 4, COL_GB)
            for j, (m, c) in enumerate(PROJB_FIRST):
                wait(sync, weight_lo_ready, Q_PROJB + j + 1 - RING)
                sync.dma_start(weight_raw[:, j % RING],
                               w_pb[c * CK * P:(c + 1) * CK * P, m * P:(m + 1) * P].rearrange("(c p) n -> p c n", p=P))\
                    .then_inc(raw_landed[j % RING], 16)
            for w, q0, first in ((w_pb, Q_PROJB, 1), (w_out, Q_OUT, 0)):
                with sync.Fori(first, DT // 2) as i:
                    for m in range(2):
                        tile(w, i * 2 + m, rounds(i, 8, q0), 4 * m)
            sync.wait_ge(normed, 1)
            sync.dma_start(y_prompt[LATE[0]], z[:, LATE[0]]).then_inc(stored, 16)
            _, late, cols = POOL_PARTS[0]
            sync.wait_ge(normed, 2)
            sync.dma_start(y_prompt[late][:, 0:D // 2], z[:, late, 0:D // 2]).then_inc(stored, 16)
            sync.wait_ge(pool_normed, 1)
            sync.dma_start(y_prompt[late][:, cols], z[:, late, cols]).then_inc(stored, 16)
            for n in range(2 * len(EARLY)):
                t, cols = n // 2, slice(n % 2 * D // 2, (n % 2 + 1) * D // 2)
                sync.wait_ge(y_ready, n + 1)
                sync.dma_start(y_prompt[t][:, cols], z[:, t, cols]).then_inc(stored, 16)
            sync.wait_ge(stored, 16 * STORES)
            sync.wait_ge(rows_stored, 16 * ROW_STORES)

        @block.gpsimd
        def _(pool):
            def spill(m, slot, src, ready, dram, done):
                pool.wait_ge(ready, m + 1)
                pool.dma_start(dram[ds(m, 1)].rearrange("o p n -> (o p) n"), src[slot][:, :]).then_inc(done[slot], 16)

            pool.dma_start(counts[:, :], host["reciprocals"]).then_inc(consts_landed, 16)
            for row, name in ((CONV_W, "conv_w"), (CONV_B, "conv_b"), (LRU_BA, "lru_ba"), (LRU_BX, "lru_bx"), (LRU_L, "lru_L")):
                v = a[name].rearrange("o (n p) -> (o n) p", p=P) if len(a[name].shape) == 2 else \
                    a[name].rearrange("o k (n p) -> (o k n) p", p=P)
                pool.dma_start(chan_rows[row:row + v.shape[0], :], v).then_inc(consts_landed, 16)
            pool.dma_start(bias_rows[0:2 * DT, :], a["b_merge"].rearrange("o k (n p) -> (o k n) p", p=P)).then_inc(consts_landed, 16)
            pool.dma_start(bias_rows[2 * DT:, :], a["pool_scale"].rearrange("o (n p) -> (o n) p", p=P)).then_inc(consts_landed, 16)

            with pool.Fori(0, DT // 2) as i:
                for m in range(2):
                    spill(i * 2 + m, m, gate_out, gate_tanh_ready, gate_b_dram, gate_spilled)

            pool.wait_ge(setup_taken, SETUP_BANKS)
            for b in pool_ext:
                pool.memset(b[:, 0:HIST], 0.0).then_inc(pads_zero, 1)

            def pool_group(g):
                wait(pool, pw_lo_ready, g)
                pool.dma_start(pw_raw[:], a["pool_w"][0][ds(g, 1)].rearrange("o (k p) n -> p (o k) n", p=P))\
                    .then_inc(pw_landed, 16)
                for u in range(2):
                    wait(pool, diff_ready, g * 2 + (u - 1))
                    wait(pool, rows_kept, g * 2 + (u - 1))
                    pool.tensor_copy(pool_seg(pool_ext[u], 0, HIST),
                                     pool_hist[:, ds(g * 2 + u, 1), :].rearrange("p o (b s) -> p (o b) s", s=HIST))\
                        .then_inc(hist_in, 1)
                for u in range(2):
                    pool.wait_ge(ext_ready, g * 2 + (u + 1))
                    kept = pool_rows[:, :, ds(g * 2 + u, 1)]
                    pool.tensor_copy(kept[:, 0:HIST], pool_ext[u][:, SEQ:SEQ + HIST].rearrange("p (s o) -> p s o", o=1))
                    pool.tensor_copy(kept[:, HIST:].rearrange("p (b s) o -> p b (s o)", s=NEW),
                                     pool_seg(pool_ext[u], HIST, NEW)).then_inc(rows_kept, 1)

            pool_group(0)
            with pool.Fori(1, GROUPS) as g:
                pool_group(g)

            with pool.Fori(0, DT // 2) as i:
                for m in range(2):
                    spill(i * 2 + m, m, part_out, part_ready, part_a_dram, part_spilled)

            for s in (*gate_spilled, *part_spilled):
                pool.wait_ge(s, 16 * DT // 2)
            pool.memset(conv_ext[:, 0:CH], 0.0).then_inc(pads_zero, 1)

            def keep_h(n):
                pool.wait_ge(h_ready, n + 1)
                kept = h_rows[:, :, ds(n, 1)]
                pool.tensor_copy(kept[:, 0:1], half_tanh[:, SEQ - 1:SEQ].rearrange("p (s o) -> p s o", o=1))
                pool.tensor_copy(kept[:, 1:SROWS], conv_seg(half_tanh, NEW - 1, 1)).then_inc(h_kept, 1)

            def lru_block(n, before):
                wait(pool, small_lo_ready, n)
                for k, w in enumerate((a["lru_wa"], a["lru_wx"])):
                    pool.dma_start(small_raw[:, k], w[0][ds(n, 1)].rearrange("o p n -> (o p) n"))\
                        .then_inc(small_landed, 16)
                wait(pool, tap_done[TAPS - 1], n)
                wait(pool, conv_rows_kept, n)
                pool.tensor_copy(conv_seg(conv_ext, 0, CH),
                                 conv_hist[:, ds(n, 1), :].rearrange("p o (b s) -> p (o b) s", s=CH))\
                    .then_inc(conv_hist_in, 1)
                if before is not None:
                    keep_h(before)
                pool.wait_ge(conv_ext_ready, n + 1)
                kept = conv_rows[:, :, ds(n, 1)]
                pool.tensor_copy(kept[:, 0:CH], conv_ext[:, SEQ:SEQ + CH].rearrange("p (s o) -> p s o", o=1))
                pool.tensor_copy(kept[:, CH:].rearrange("p (b s) o -> p b (s o)", s=CH),
                                 conv_seg(conv_ext, NEW, CH)).then_inc(conv_rows_kept, 1)

            lru_block(0, None)
            with pool.Fori(1, BLOCKS) as n:
                lru_block(n, n - 1)

            keep_h(BLOCKS - 1)
            pool.wait_ge(lru_done, BLOCKS)
            pool.wait_ge(conv_rows_kept, BLOCKS)
            pool.wait_ge(half_ready, BLOCKS)

            def merge_inputs(i):
                for m in range(2):
                    wait(pool, merge_ready, i * 2 + (m - 1))
                    pool.dma_start(gate_in[m][:, :], gate_b_dram[ds(i * 2 + m, 1)].rearrange("o p n -> (o p) n"))\
                        .then_inc(gate_loaded[m], 16)
                    pool.dma_start(part_in[m][:, :], part_a_dram[ds(i * 2 + m, 1)].rearrange("o p n -> (o p) n"))\
                        .then_inc(gate_loaded[m], 16)

            merge_inputs(0)
            merge_inputs(1)
            pool.wait_ge(rows_ready, 3)
            rows = lambda b, c: rows_sb[:, b, c * P:(c + 1) * P]
            per = P // PT_ // NEW
            pool_new = out[5][0][:, HIST - NEW:, :].rearrange("b s (j p) -> b s j p", p=P)
            for b in range(NSEQ):
                src = rows(0, b // per)[b % per * NEW * PT_:(b % per + 1) * NEW * PT_, :]
                pool.dma_start(pool_new[b].rearrange("s j p -> (s j) p"), src).then_inc(rows_stored, 16)
            pool.dma_start(out[2][0].rearrange("b s (j p) -> (b s j) p", p=P), rows(1, 0)[0:HIST * PT_, :]).then_inc(rows_stored, 16)
            pool.dma_start(out[4][0].rearrange("b (j p) -> (b j) p", p=P), rows(1, 1)[0:DT, :]).then_inc(rows_stored, 16)
            pool.dma_start(out[7][0].rearrange("b (j p) -> (b j) p", p=P), rows(1, 2)[0:NSEQ * DT, :]).then_inc(rows_stored, 16)
            pool.dma_start(out[3][0].rearrange("b s (j p) -> (b s j) p", p=P), rows(2, 3)[0:CH * DT, :]).then_inc(rows_stored, 16)
            conv_new = out[6][0].rearrange("b s (j p) -> (b s j) p", p=P)
            for c in range(3):
                pool.dma_start(conv_new[c * P:(c + 1) * P, :], rows(2, c)).then_inc(rows_stored, 16)
            with pool.Fori(2, DT // 2) as i:
                merge_inputs(i)

            pool.wait_ge(chunk_done, Q_OUT)
            pool.memset(scale_raw[0:SHIFT_ROWS, :], 0.0).then_inc(rows_zero, 1)
            for t in range(XT):
                pool.dma_start(z[:, t], x_prompt[t]).then_inc(z_loaded, 16)
            pool.dma_start(z[0:SAMP, XT], x_sample).then_inc(z_loaded, 16)
            pool.dma_start(gamma[:, :], a["ln_g"].partition_broadcast(P)).then_inc(z_loaded, 16)
            pool.dma_start(beta[:, :], a["ln_b"].partition_broadcast(P)).then_inc(z_loaded, 16)
            pool.wait_ge(rows_zero, 1)
            for row in range(0, SHIFT_ROWS, 32):
                pool.dma_start(scale_raw[row:row + 1, :], a["ln_g"]).then_inc(scale_loaded, 16)
                pool.dma_start(scale_raw[row + 1:row + 2, :], a["ln_b"]).then_inc(scale_loaded, 16)
            for n, (rows, t, cols) in enumerate(POOL_PARTS):
                part = z[0:rows, t, cols]
                pool.wait_ge(centred, n + 1)
                pool.tensor_tensor(part, part, gamma[0:rows, cols], ALU.mult).then_inc(pool_scaled, 1)
                pool.wait_ge(pool_scaled, n + 1)
                pool.tensor_tensor(part, part, beta[0:rows, cols], ALU.add).then_inc(pool_normed, 1)

        @block.scalar
        def _(act):
            def split(r, j, hi=weight_hi):
                act.wait_ge(raw_landed[j % RING], r * 16 + 16 * (j // RING + 1))
                if hi is weight_hi:
                    wait(act, chunk_done, r * RING + (j + 1 - RING))
                act.activation(hi[:, j % RING], weight_raw[:, j % RING], ACT.Copy).then_inc(weight_hi_ready, 1)

            def steps(r, per, tail, own):
                for j in range(per):
                    split(r, j + 3)
                    tail(j)
                    own(j)

            act.dma_start(ident[:, :], host["identity"]).then_inc(ident_landed, 16)

            def round_x(s):
                c, t, n = x_step(s)
                act.wait_ge(setup_turned, s + 1)
                act.activation(xh[:, CK * c:CK * c + CK, t * P:t * P + n],
                               setup_bank(s)[:, 0:CK * n].rearrange("p (k n) -> p k n", n=n), ACT.Copy).then_inc(setup_hi, 1)

            setup_order(round_x, lambda q: split(0, q), SPLIT_BEFORE)
            act.wait_ge(param_step, 1)
            act.activation(sp[1][:, :], sp[0][:, :], ACT.Exp, scale=-1.0).then_inc(param_exp, 1)
            for j in range(RING - 1):
                split(0, PER_GATE + j)

            act.wait_ge(params_ready, 1)

            def gate_tanh(i, m, r, j):
                act.wait_ge(chunk_done, r * RING + j)
                wait(act, gate_spilled[m], i * 16)
                act.activation(halves(gate_out[m][:, :]), pair(m), ACT.Tanh, bias=gate_col(1, i * 2 + m), scale=0.5)\
                    .then_inc(gate_tanh_ready, 1)

            def gate_tail(i, r):
                def tail(j):
                    if j == 0:
                        gate_tanh(i, 1, r, 0)
                return tail

            def gate(i, tail):
                r = rounds(i, PER_GATE, Q_GATE)
                steps(r, PER_GATE, tail, lambda j: gate_tanh(i, 0, r, 4) if j == 4 else None)

            gate_tanh(0, 0, 0, PER_GATE - 1)
            with act.Fori(1, DT // 2) as i:
                gate(i, gate_tail(i - 1, rounds(i, PER_GATE, Q_GATE)))

            def pool_copy(g, u, r):
                e = pool_ext[u]
                act.wait_ge(chunk_done, r * RING + 4 * (u + 1))
                act.wait_ge(hist_in, g * 2 + (u + 1))
                act.activation(e[:, HIST:HIST + TH], ps[:, 2 * u, 0:TH], ACT.Copy)
                act.activation(e[:, HIST + TH:HIST + SEQ], ps[:, 2 * u + 1, 0:SEQ - TH], ACT.Copy)
                act.activation(pool_seg(e, HIST, NEW), sample_cols(ps[:, 2 * u + 1, SEQ - TH:TH]), ACT.Copy)\
                    .then_inc(ext_ready, 1)

            def diff_round(g, u):
                act.wait_ge(diff_ready, g * 2 + (u + 1))
                wait(act, mixed_done, g * 2)
                act.activation(dfh[:, u], diff[:, :], ACT.Copy).then_inc(diff_hi, 1)

            def pool_tanh_of(g, u, r, j):
                act.wait_ge(chunk_done, r * RING + j)
                wait(act, pool_silu_ready, g * 2 + u)
                act.activation(halves(pool_tanh[:, :]), pair(2 + u), ACT.Tanh, scale=0.5).then_inc(pool_tanh_ready, 1)

            def ya_round(g, u):
                act.wait_ge(ya_ready, g * 2 + (u + 1))
                act.activation(yah[:, ds(g * 2 + u, 1), :].rearrange("p o n -> p (o n)"), y_a[:, :], ACT.Copy).then_inc(ya_hi, 1)

            def pool_tail(g, r):
                def tail(j):
                    if j == 0:
                        pool_tanh_of(g, 1, r, 0)
                    if j == 2:
                        ya_round(g, 1)
                return tail

            def pool_group(g, tail):
                r = rounds(g, PER_POOL, Q_POOL)

                def own(j):
                    if j == 4:
                        pool_copy(g, 0, r)
                    if j == 6:
                        diff_round(g, 0)
                    if j == 7:
                        act.wait_ge(pw_landed, g * 16 + 16)
                        wait(act, mixed_done, g * 2)
                        act.activation(pw_hi[:], pw_raw[:], ACT.Copy).then_inc(pw_hi_ready, 1)
                    if j == 8:
                        pool_copy(g, 1, r)
                    if j == 10:
                        diff_round(g, 1)
                    if j == 12:
                        pool_tanh_of(g, 0, r, 12)
                    if j == 14:
                        ya_round(g, 0)
                steps(r, PER_POOL, tail, own)

            pool_group(0, gate_tail(DT // 2 - 1, Q_POOL // RING))
            with act.Fori(1, GROUPS) as g:
                pool_group(g, pool_tail(g - 1, rounds(g, PER_POOL, Q_POOL)))

            def proj_a(i, tail):
                r = rounds(i, PER_PROJA, Q_PROJA)

                def own(j):
                    if j in (4, 8):
                        m = j // 4 - 1
                        act.wait_ge(chunk_done, r * RING + j)
                        wait(act, part_ready, i * 2 + (m - 1))
                        act.activation(halves(ma_tanh[m][:, :]), pair(m), ACT.Tanh, bias=gate_col(0, i * 2 + m), scale=0.5)\
                            .then_inc(ma_tanh_ready, 1)
                steps(r, PER_PROJA, tail, own)

            proj_a(0, pool_tail(GROUPS - 1, Q_PROJA // RING))
            with act.Fori(1, DT // 2) as i:
                proj_a(i, lambda j: None)

            def lru_tail(n, r):
                def tail(j):
                    if j == 0:
                        act.wait_ge(chunk_done, r * RING)
                        wait(act, yb_lo, n)
                        act.activation(halves(gb_tanh[:, :]), pair(1), ACT.Tanh, scale=0.5).then_inc(gb_tanh_ready, 1)
                        act.wait_ge(lru_done, n + 1)
                        act.activation(r_tanh[:, 0:XE].rearrange("p (h n) -> p h n", h=2), pair(2, XEH), ACT.Tanh,
                                       bias=bias_ri[:, ds(n, 1)], scale=0.5).then_inc(r_ready, 1)
                        wait(act, h_ready, n)
                        act.activation(i_tanh[:, 0:XE].rearrange("p (h n) -> p h n", h=2), pair(3, XEH), ACT.Tanh,
                                       bias=bias_ri[:, ds(n + DT, 1)], scale=0.5).then_inc(i_ready, 1)
                    if j == 1:
                        act.wait_ge(r_ready, n + 1)
                        act.activation(decay[:, 0:XE], r_tanh[:, 0:XE], ACT.Exp,
                                       bias=neg_c2[:, ds(n, 1)], scale=neg_c2[:, ds(n, 1)]).then_inc(exp_ready, 1)
                        wait(act, yb_ready, n)
                        wait(act, h_kept, n)
                        act.activation(half_tanh[:, 0:XE], r_tanh[:, 0:XE], ACT.Tanh,
                                       bias=pos_c4[:, ds(n, 1)], scale=pos_c4[:, ds(n, 1)]).then_inc(half_ready, 1)
                    if j == 2:
                        wait(act, drive_ready, n)
                        act.wait_ge(half_ready, n + 1)
                        act.activation(root[:, 0:XE], half_tanh[:, 0:XE], ACT.Sqrt, scale=0.25).then_inc(root_ready, 1)
                    if j == 3:
                        act.wait_ge(yb_ready, n + 1)
                        act.activation(ybh[:, ds(n, 1), :].rearrange("p o n -> p (o n)"), gb_tanh[:, :], ACT.Copy).then_inc(yb_hi, 1)
                return tail

            def lru(n, tail):
                r = rounds(n, PER_LRU, Q_LRU)

                def own(j):
                    if j == 4:
                        e = conv_ext
                        act.wait_ge(chunk_done, r * RING + 4)
                        act.wait_ge(conv_hist_in, n + 1)
                        act.activation(e[:, CH:CH + TH], ps[:, 0, 0:TH], ACT.Copy)
                        act.activation(e[:, CH + TH:CH + SEQ], ps[:, 1, 0:SEQ - TH], ACT.Copy)
                        act.activation(conv_seg(e, CH, NEW), sample_cols(ps[:, 1, SEQ - TH:TH]), ACT.Copy)\
                            .then_inc(conv_ext_ready, 1)
                    if j == 5:
                        act.wait_ge(tap_done[TAPS - 1], n + 1)
                        wait(act, lru_done, n)
                        act.activation(conv_x_hi[:, 0:XE], conv_x[:, 0:XE], ACT.Copy).then_inc(conv_hi, 1)
                    if j == 6:
                        act.wait_ge(small_landed, n * 32 + 32)
                        wait(act, lru_done, n)
                        act.activation(small_hi[:], small_raw[:], ACT.Copy).then_inc(small_hi_ready, 1)
                steps(r, PER_LRU, tail, own)

            lru(0, lambda j: None)
            with act.Fori(1, BLOCKS) as n:
                lru(n, lru_tail(n - 1, rounds(n, PER_LRU, Q_LRU)))

            def merge_round(m):
                act.wait_ge(merge_ready, m + 1)
                act.activation(xh[:, ds(m, 1), :].rearrange("p o n -> p (o n)"), merged[:, :], ACT.Copy, scale=0.5).then_inc(merged_hi, 1)

            def merge_tail(i):
                return lambda j: merge_round(i * 2 + 1) if j == 1 else None

            def proj_b(i, tail, merge_at=5):
                steps(rounds(i, PER_PROJB, Q_PROJB), PER_PROJB, tail, lambda j: merge_round(i * 2) if j == merge_at else None)

            proj_b(0, lru_tail(BLOCKS - 1, Q_PROJB // RING), PER_PROJB - 1)
            act.wait_ge(rows_turned, 1)
            for b in range(3):
                act.activation(rows_sb[:, b], ps[:, 4 + b], ACT.Copy).then_inc(rows_ready, 1)
            with act.Fori(1, DT // 2) as i:
                proj_b(i, merge_tail(i - 1))

            def out_copy(i, m, r, j):
                act.wait_ge(chunk_done, r * RING + j)
                wait(act, out_turned, i * 2 + (m - 1))
                act.activation(halves(out_sb[m][:, :]), pair(m), ACT.Copy).then_inc(out_copied, 1)

            def out_tail(i, r):
                return lambda j: out_copy(i, 1, r, 0) if j == 0 else None

            def project(i, tail):
                r = rounds(i, PER_OUT, Q_OUT)
                steps(r, PER_OUT, tail, lambda j: out_copy(i, 0, r, 4) if j == 4 else None)

            project(0, merge_tail(DT // 2 - 1))
            with act.Fori(1, DT // 2 - 1) as i:
                project(i, out_tail(i - 1, rounds(i, PER_OUT, Q_OUT)))
            act.wait_ge(scale_loaded, 16 * 6)
            act.activation(scale_rows[0:SHIFT_ROWS, :], scale_raw[0:SHIFT_ROWS, :], ACT.Copy).then_inc(scale_hi, 1)
            r = Q_END // RING - 2
            split(r, RING - 1)
            out_copy(DT // 2 - 2, 1, r, 0)
            act.wait_ge(rows_stored, 16 * ROW_STORES)
            for j in range(RING, PER_OUT):
                split(r, j, more_hi)
            for m in range(2):
                act.wait_ge(chunk_done, r * RING + 4 * (m + 1))
                act.wait_ge(out_turned, DT - 3 + m)
                act.activation(out_sb[m][:, TE:T], ps[:, 2 * m, 0:TL], ACT.Copy).then_inc(out_copied, 1)

            def deviation(n):
                act.wait_ge(var_ready, n)
                tiles = LATE if n == 1 else EARLY
                sl = slice(tiles[0], tiles[-1] + 1)
                act.activation(rstd[1][:, sl], rstd[0][:, sl], ACT.Sqrt).then_inc(root_var, 1)

            def early_copy(m):
                act.wait_ge(early_done, m + 1)
                act.activation(out_sb[m][:, 0:TE], ps[:, 2 * m + 1, 0:TE], ACT.Copy).then_inc(out_copied, 1)

            deviation(1)
            early_copy(0)
            act.wait_ge(shift_ready, 1)
            for rows, t, cols in POOL_PARTS:
                act.activation(z[0:rows, t, cols], z[0:rows, t, cols], ACT.Identity, bias=rstd[3][0:rows, t:t + 1],
                               scale=rstd[2][0:rows, t:t + 1]).then_inc(centred, 1)
            early_copy(1)
            deviation(2)
            act.wait_ge(shift_turned, 1)
            act.activation(shift_rows[0:SHIFT_ROWS, :, :].rearrange("p t n -> p (t n)"), ps[0:SHIFT_ROWS, 0, 0:TE], ACT.Copy).then_inc(shift_hi, 1)
            act.wait_ge(pool_normed, 2)
            act.dma_start(y_sample, z[0:SAMP, XT]).then_inc(stored, 16)

        @block.vector
        def _(dve):
            def split(r, j, hi=weight_hi, lo=weight_lo):
                dve.wait_ge(weight_hi_ready, r * RING + (j + 1))
                dve.tensor_tensor(lo[:, j % RING], weight_raw[:, j % RING], f32(hi[:, j % RING]),
                                  ALU.subtract).then_inc(weight_lo_ready, 1)

            def steps(r, per, tail, own):
                for j in range(per):
                    split(r, j + 3)
                    tail(j)
                    own(j)

            def rest_x(s):
                c, t, n = x_step(s)
                cols = slice(t * P, t * P + n)
                dve.wait_ge(setup_hi, s + 1)
                dve.tensor_tensor(xl[:, CK * c:CK * c + CK, cols], setup_bank(s)[:, 0:CK * n].rearrange("p (k n) -> p k n", n=n),
                                  f32(xh[:, CK * c:CK * c + CK, cols]), ALU.subtract).then_inc(setup_taken, 1)

            setup_order(rest_x, lambda q: split(0, q), SPLIT_BEFORE)
            dve.wait_ge(setup_turned, X_BANKS + 1)
            src = setup_bank(X_BANKS)
            dve.tensor_copy(chan[:, :], src[:, 0:P])
            dve.tensor_scalar(bias_m[:, :], src[:, P:P + 2 * DT + PT_], 0.5, None, ALU.mult).then_inc(setup_taken, 1)
            count = 0

            def param(ins):
                nonlocal count
                count += 1
                ins.then_inc(param_step, 1)
                dve.wait_ge(param_step, count)

            dve.wait_ge(setup_taken, X_BANKS + 1)
            L, (absL, t_exp, u, u2, w) = chan[:, LRU_L:LRU_L + DT], [x[:, :] for x in sp]
            param(dve.scalar_tensor_tensor(out=absL, in0=L, scalar=-1.0, in1=L, op0=ALU.mult, op1=ALU.max))
            param(dve.tensor_scalar(bias_ri[:, :], chan[:, LRU_BA:LRU_BA + 2 * DT], 0.5, None, ALU.mult))
            dve.wait_ge(param_exp, 1)
            param(dve.tensor_scalar(w, t_exp, 2.0, None, ALU.add))
            param(dve.reciprocal(u2, w))
            param(dve.tensor_tensor(u, t_exp, u2, ALU.mult))
            param(dve.tensor_tensor(u2, u, u, ALU.mult))
            param(dve.tensor_scalar(w, u2, 1.0 / 15, None, ALU.mult))
            for k in (13, 11, 9, 7, 5, 3):
                param(dve.scalar_tensor_tensor(out=w, in0=w, scalar=1.0 / k, in1=u2, op0=ALU.add, op1=ALU.mult))
            param(dve.scalar_tensor_tensor(out=w, in0=w, scalar=1.0, in1=u, op0=ALU.add, op1=ALU.mult))
            param(dve.tensor_scalar(u, L, -1.0, 0.0, ALU.mult, ALU.max))
            param(dve.scalar_tensor_tensor(out=w, in0=w, scalar=2.0, in1=u, op0=ALU.mult, op1=ALU.add))
            param(dve.tensor_scalar(neg_c2[:, :], w, -4.0, None, ALU.mult))
            dve.tensor_scalar(pos_c4[:, :], w, 2.0, None, ALU.mult).then_inc(params_ready, 1)
            for j in range(RING - 1):
                split(0, PER_GATE + j)
            for k, (dst, n) in enumerate(((conv_hist[:, :, :], DT * NSEQ * CH), (h_init[:, :, :], DT * NSEQ),
                                          (pool_hist[:, 0:4, :], 4 * NSEQ * HIST), (pool_hist[:, 4:8, :], 4 * NSEQ * HIST))):
                dve.wait_ge(setup_turned, X_BANKS + 2 + k)
                dve.tensor_copy(dst.rearrange("p n s -> p (n s)"), setup_bank(X_BANKS + 1 + k)[:, 0:n]).then_inc(setup_taken, 1)

            none = lambda j: None
            with dve.Fori(1, DT // 2) as i:
                steps(rounds(i, PER_GATE, Q_GATE), PER_GATE, none, none)

            stepped = 0

            def window_op(ins):
                nonlocal stepped
                stepped += 1
                ins.then_inc(window_step, 1)
                dve.wait_ge(window_step, stepped)

            def pool_diff(g, u):
                e, W = pool_ext[u], WIDTHS[g]
                dve.wait_ge(ext_ready, g * 2 + u + 1)
                dve.wait_ge(pads_zero, 2)
                src, w = e, 1
                while w < W:
                    dst = window[0] if src is not window[0] else window[1]
                    window_op(dve.tensor_tensor(dst[:, 2 * w - 1:PEXT], src[:, 2 * w - 1:PEXT], src[:, w - 1:PEXT - w], ALU.add))
                    src, w = dst, 2 * w
                spare = window[0] if src is window[1] else window[1]
                window_op(dve.tensor_tensor(spare[:, 0:W - 1], src[:, HIST:HIST + W - 1], counts[:, 0:W - 1], ALU.mult))
                dve.tensor_tensor(diff[:, 0:W - 1], spare[:, 0:W - 1], e[:, HIST:HIST + W - 1], ALU.subtract)
                dve.scalar_tensor_tensor(out=diff[:, W - 1:SEQ], in0=src[:, HIST + W - 1:HIST + SEQ], scalar=1.0 / W,
                                         in1=e[:, HIST + W - 1:HIST + SEQ], op0=ALU.mult, op1=ALU.subtract)
                dve.scalar_tensor_tensor(out=sample_cols(diff[:, SEQ:T]), in0=pool_seg(src, HIST, NEW), scalar=1.0 / W,
                                         in1=pool_seg(e, HIST, NEW), op0=ALU.mult, op1=ALU.subtract).then_inc(diff_ready, 1)

            def diff_rest(g, u):
                dve.wait_ge(diff_hi, g * 2 + u + 1)
                dve.tensor_tensor(dfl[:, u], diff[:, :], f32(dfh[:, u]), ALU.subtract).then_inc(diff_lo, 1)

            def pool_silu_of(g, u):
                dve.wait_ge(pool_tanh_ready, g * 2 + u + 1)
                dve.scalar_tensor_tensor(out=halves(pool_silu[u][:, :]), in0=halves(pool_tanh[:, :]), scalar=1.0,
                                         in1=pair(2 + u), op0=ALU.add, op1=ALU.mult).then_inc(pool_silu_ready, 1)

            def ya(g, u):
                dve.wait_ge(mixed_done, g * 2 + u + 1)
                dve.wait_ge(pool_silu_ready, g * 2 + u + 1)
                dve.wait_ge(ya_hi, g * 2 + u) if g * 2 + u else None
                dve.scalar_tensor_tensor(out=halves(y_a[:, :]), in0=pair(u), scalar=bias_m[:, 2 * DT + 2 * g + u:2 * DT + 2 * g + u + 1],
                                         in1=halves(pool_silu[u][:, :]), op0=ALU.mult, op1=ALU.mult).then_inc(ya_ready, 1)

            def ya_rest(g, u):
                dve.wait_ge(ya_hi, g * 2 + u + 1)
                dve.tensor_tensor(yal[:, 2 * g + u], y_a[:, :], f32(yah[:, 2 * g + u]), ALU.subtract).then_inc(ya_lo, 1)

            def pool_tail(g):
                def tail(j):
                    if j == 0:
                        pool_silu_of(g, 1)
                    if j == 1:
                        ya(g, 1)
                    if j == 2:
                        ya_rest(g, 1)
                return tail

            def pool_group(g, tail):
                def own(j):
                    if j == 4:
                        pool_diff(g, 0)
                    if j == 6:
                        diff_rest(g, 0)
                    if j == 7:
                        dve.wait_ge(pw_hi_ready, g + 1)
                        dve.tensor_tensor(pw_lo[:], pw_raw[:], f32(pw_hi[:]), ALU.subtract).then_inc(pw_lo_ready, 1)
                    if j == 8:
                        pool_diff(g, 1)
                    if j == 10:
                        diff_rest(g, 1)
                    if j == 12:
                        pool_silu_of(g, 0)
                    if j == 13:
                        ya(g, 0)
                    if j == 14:
                        ya_rest(g, 0)
                steps(rounds(g, PER_POOL, Q_POOL), PER_POOL, tail, own)

            for g in range(GROUPS):
                pool_group(g, pool_tail(g - 1) if g else none)

            def part(i, m, r, j):
                dve.wait_ge(chunk_done, r * RING + j)
                dve.wait_ge(ma_tanh_ready, i * 2 + (m + 1))
                wait(dve, part_spilled[m], i * 16)
                dve.scalar_tensor_tensor(out=halves(part_out[m][:, :]), in0=halves(ma_tanh[m][:, :]), scalar=1.0,
                                         in1=pair(2 + m), op0=ALU.add, op1=ALU.mult).then_inc(part_ready, 1)

            def part_tail(i, r):
                return lambda j: part(i, 1, r, 0) if j == 0 else None

            def proj_a(i, tail):
                r = rounds(i, PER_PROJA, Q_PROJA)
                steps(r, PER_PROJA, tail, lambda j: part(i, 0, r, 10) if j == 10 else None)

            proj_a(0, pool_tail(GROUPS - 1))
            with dve.Fori(1, DT // 2) as i:
                proj_a(i, part_tail(i - 1, rounds(i, PER_PROJA, Q_PROJA)))

            def lru_tail(n):
                X = slice(0, XE)

                def tail(j):
                    if j == 0:
                        dve.wait_ge(gb_tanh_ready, n + 1)
                        dve.scalar_tensor_tensor(out=halves(gb_silu[:, :]), in0=halves(gb_tanh[:, :]), scalar=1.0,
                                                 in1=pair(1), op0=ALU.add, op1=ALU.mult).then_inc(gb_silu_ready, 1)
                    if j == 1:
                        dve.wait_ge(i_ready, n + 1)
                        dve.scalar_tensor_tensor(out=i_tanh[:, X], in0=i_tanh[:, X], scalar=1.0, in1=conv_x[:, X],
                                                 op0=ALU.add, op1=ALU.mult).then_inc(ix_ready, 1)
                        dve.wait_ge(exp_ready, n + 1)
                        dve.wait_ge(half_ready, n + 1)
                        dve.scalar_tensor_tensor(out=decay[:, X], in0=decay[:, X], scalar=1.0, in1=half_tanh[:, X],
                                                 op0=ALU.add, op1=ALU.mult).then_inc(fall_ready, 1)
                        dve.wait_ge(fall_ready, n + 1)
                        dve.tensor_scalar(decay[:, X], decay[:, X], -1.0, 1.0, ALU.mult, ALU.add).then_inc(decay_ready, 1)
                    if j == 2:
                        dve.wait_ge(root_ready, n + 1)
                        dve.wait_ge(decay_ready, n + 1)
                        dve.scalar_tensor_tensor(out=root[:, X], in0=decay[:, X], scalar=1.0, in1=root[:, X],
                                                 op0=ALU.add, op1=ALU.mult).then_inc(scale_ready, 1)
                        dve.wait_ge(scale_ready, n + 1)
                        dve.wait_ge(ix_ready, n + 1)
                        dve.tensor_tensor(i_tanh[:, X], root[:, X], i_tanh[:, X], ALU.mult).then_inc(drive_ready, 1)
                        dve.tensor_tensor(start_term[:, :].rearrange("p (b o) -> p b o", o=1), conv_seg(decay, 0, 1),
                                          h_init[:, ds(n, 1), :].rearrange("p o b -> p b o"), ALU.mult).then_inc(start_ready, 1)
                        dve.wait_ge(drive_ready, n + 1)
                        dve.wait_ge(start_ready, n + 1)
                        dve.tensor_tensor(conv_seg(i_tanh, 0, 1), conv_seg(i_tanh, 0, 1),
                                          start_term[:, :].rearrange("p (b o) -> p b o", o=1), ALU.add)
                        dve.memset(conv_seg(decay, 0, 1), 0.0).then_inc(decay_cut, 1)
                    if j == 3:
                        dve.wait_ge(decay_cut, n + 1)
                        dve.tensor_tensor_scan(half_tanh[:, X], decay[:, X], i_tanh[:, X], 0.0, ALU.mult, ALU.add).then_inc(h_ready, 1)
                        dve.wait_ge(h_ready, n + 1)
                        dve.wait_ge(gb_silu_ready, n + 1)
                        dve.scalar_tensor_tensor(out=gb_tanh[:, 0:SEQ], in0=half_tanh[:, 0:SEQ], scalar=0.5, in1=gb_silu[:, 0:SEQ],
                                                 op0=ALU.mult, op1=ALU.mult)
                        dve.scalar_tensor_tensor(out=sample_cols(gb_tanh[:, SEQ:T]), in0=conv_seg(half_tanh, 0, NEW), scalar=0.5,
                                                 in1=sample_cols(gb_silu[:, SEQ:T]), op0=ALU.mult, op1=ALU.mult).then_inc(yb_ready, 1)
                        dve.wait_ge(yb_hi, n + 1)
                        dve.tensor_tensor(ybl[:, ds(n, 1), :].rearrange("p o n -> p (o n)"), gb_tanh[:, :],
                                          f32(ybh[:, ds(n, 1), :].rearrange("p o n -> p (o n)")), ALU.subtract).then_inc(yb_lo, 1)
                return tail

            def lru(n, tail):
                def own(j):
                    if j == 4:
                        dve.wait_ge(conv_ext_ready, n + 1)
                        dve.wait_ge(pads_zero, 3)
                        dve.tensor_scalar(conv_x[:, 0:XE], conv_ext[:, 0:XE], chan[:, ds(n + CONV_W, 1)], chan[:, ds(n + CONV_B, 1)],
                                          ALU.mult, ALU.add).then_inc(tap_done[0], 1)
                        for k in range(1, TAPS):
                            dve.wait_ge(tap_done[k - 1], n + 1)
                            dve.scalar_tensor_tensor(out=conv_x[:, 0:XE], in0=conv_ext[:, k:k + XE], scalar=chan[:, ds(n + (CONV_W + k * DT), 1)],
                                                     in1=conv_x[:, 0:XE], op0=ALU.mult, op1=ALU.add).then_inc(tap_done[k], 1)
                    if j == 6:
                        dve.wait_ge(conv_hi, n + 1)
                        dve.tensor_tensor(conv_x_lo[:, 0:XE], conv_x[:, 0:XE], f32(conv_x_hi[:, 0:XE]), ALU.subtract).then_inc(conv_lo, 1)
                        dve.wait_ge(small_hi_ready, n + 1)
                        dve.tensor_tensor(small_lo[:], small_raw[:], f32(small_hi[:]), ALU.subtract).then_inc(small_lo_ready, 1)
                steps(rounds(n, PER_LRU, Q_LRU), PER_LRU, tail, own)

            lru(0, part_tail(DT // 2 - 1, Q_LRU // RING))
            with dve.Fori(1, BLOCKS) as n:
                lru(n, lru_tail(n - 1))

            def merge(i, m, r, j):
                dve.wait_ge(chunk_done, r * RING + j)
                dve.wait_ge(gate_loaded[m], i * 32 + 32)
                wait(dve, merged_lo, i * 2 + m)
                dve.scalar_tensor_tensor(out=halves(merged[:, :]), in0=halves(gate_in[m][:, :]), scalar=1.0, in1=pair(m),
                                         op0=ALU.add, op1=ALU.mult).then_inc(gated_ready, 1)
                dve.wait_ge(gated_ready, i * 2 + (m + 1))
                dve.tensor_tensor(merged[:, :], merged[:, :], part_in[m][:, :], ALU.add).then_inc(merge_ready, 1)

            def merge_rest(m):
                dve.wait_ge(merged_hi, m + 1)
                dve.scalar_tensor_tensor(out=xl[:, ds(m, 1), :].rearrange("p o n -> p (o n)"), in0=merged[:, :], scalar=0.5,
                                         in1=f32(xh[:, ds(m, 1), :].rearrange("p o n -> p (o n)")),
                                         op0=ALU.mult, op1=ALU.subtract).then_inc(merged_lo, 1)

            def merge_tail(i, r):
                def tail(j):
                    if j == 0:
                        merge(i, 1, r, 0)
                    if j == 1:
                        merge_rest(i * 2 + 1)
                return tail

            def proj_b(i, tail, merge_at=(4, 5)):
                r = rounds(i, PER_PROJB, Q_PROJB)

                def own(j):
                    if j == merge_at[0]:
                        merge(i, 0, r, j)
                    if j == merge_at[1]:
                        merge_rest(i * 2)
                steps(r, PER_PROJB, tail, own)

            proj_b(0, lru_tail(BLOCKS - 1), (PER_PROJB - 1, PER_PROJB - 1))
            with dve.Fori(1, DT // 2) as i:
                proj_b(i, merge_tail(i - 1, rounds(i, PER_PROJB, Q_PROJB)))

            def residual(i, m):
                tile_ = i * 2 + m
                dve.wait_ge(z_loaded, 16 * (XT + 3))
                dve.wait_ge(out_turned, tile_ + 1)
                zp = z[:, 0:XT, ds(tile_ * P, P)]
                dve.scalar_tensor_tensor(out=zp, in0=zp, scalar=ALPHA, in1=ps[:, 4 + 2 * m].rearrange("p (t n) -> p t n", n=P),
                                         op0=ALU.mult, op1=ALU.add)
                zs = z[0:SAMP, XT, ds(tile_ * P, P)]
                dve.scalar_tensor_tensor(out=zs, in0=zs, scalar=ALPHA, in1=ps[0:SAMP, 5 + 2 * m, 0:P],
                                         op0=ALU.mult, op1=ALU.add).then_inc(z_added, 1)

            def statistics(i, m):
                tile_ = i * 2 + m
                dve.wait_ge(z_added, tile_ + 1)
                for t in range(XT + 1):
                    n = P if t < XT else SAMP
                    ins = dve.bn_stats(stats[0:n, t, ds(tile_, 1), :].rearrange("p o s -> p (o s)"), z[0:n, t, ds(tile_ * P, P)])
                ins.then_inc(z_stats, 1)

            def out_tail(i):
                def tail(j):
                    if j == 2:
                        residual(i, 1)
                    if j == 3:
                        statistics(i, 1)
                return tail

            def project(i, tail):
                def own(j):
                    if j == 6:
                        residual(i, 0)
                    if j == 7:
                        statistics(i, 0)
                steps(rounds(i, PER_OUT, Q_OUT), PER_OUT, tail, own)

            project(0, merge_tail(DT // 2 - 1, Q_OUT // RING))
            dve.memset(minus_one[:], -1.0)
            dve.memset(shift_cols[:], 0.0).then_inc(preset, 1)
            dve.wait_ge(preset, 1)
            dve.memset(shift_cols[:, :, 1:34:32], 1.0).then_inc(preset, 1)
            dve.memset(moments[:], 1.0).then_inc(preset, 1)
            with dve.Fori(1, DT // 2 - 1) as i:
                project(i, out_tail(i - 1))

            def scaled(tiles, cols):
                for t in tiles:
                    ins = dve.tensor_tensor(z[:, t, cols], z[:, t, cols], gamma[:, cols], ALU.mult)
                ins.then_inc(z_scaled, 1)

            def part_residual(n, m, tiles):
                cols = slice((DT - 2 + m) * P, (DT - 1 + m) * P)
                dve.wait_ge(out_turned, n)
                full = [t for t in tiles if t < XT]
                zp = z[:, full[0]:full[-1] + 1, cols]
                ins = dve.scalar_tensor_tensor(out=zp, in0=zp, scalar=ALPHA,
                                               in1=ps[:, 4 + 2 * m, full[0] * P:(full[-1] + 1) * P].rearrange("p (t n) -> p t n", n=P),
                                               op0=ALU.mult, op1=ALU.add)
                if XT in tiles:
                    zs = z[0:SAMP, XT, cols]
                    ins = dve.scalar_tensor_tensor(out=zs, in0=zs, scalar=ALPHA, in1=ps[0:SAMP, 5 + 2 * m, 0:P],
                                                   op0=ALU.mult, op1=ALU.add)
                ins.then_inc(z_added, 1)
                dve.wait_ge(z_added, n)
                for t in tiles:
                    rows = P if t < XT else SAMP
                    ins = dve.bn_stats(stats[0:rows, t, DT - 2 + m, :], z[0:rows, t, cols])
                ins.then_inc(z_stats, 1)

            def deviations(n, tiles):
                part = slice(tiles[0], tiles[-1] + 1)
                dve.wait_ge(z_stats, DT + 2 * (n - 1))
                dve.wait_ge(preset, 3)
                for t in tiles:
                    rows = P if t < XT else SAMP
                    ins = dve.bn_aggr(moments[0:rows, t, :], stats[0:rows, t].rearrange("p m s -> p (m s)"))
                ins.then_inc(moments_ready, 1)
                dve.wait_ge(moments_ready, n)
                v, y, y2, t3 = (x[:, part] for x in (rstd[0], rstd[2], rstd[1], rstd[3]))
                dve.tensor_scalar(v, moments[:, part, 1], EPS, None, ALU.add).then_inc(var_ready, 1)
                dve.wait_ge(root_var, n)
                link(dve.reciprocal(y, y2))
                link(dve.tensor_tensor(t3, y, y, ALU.mult))
                link(dve.tensor_tensor(t3, t3, v, ALU.mult))
                link(dve.tensor_scalar(t3, t3, -0.5, 1.5, ALU.mult, ALU.add))
                link(dve.tensor_tensor(y, y, t3, ALU.mult))

            norm = 0

            def link(ins):
                nonlocal norm
                norm += 1
                ins.then_inc(norm_step, 1)
                dve.wait_ge(norm_step, norm)

            dve.wait_ge(scale_hi, 1)
            low = slice(32, 34)
            dve.tensor_tensor(scale_rows[low, :], scale_raw[low, :], f32(scale_rows[low, :]), ALU.subtract).then_inc(scale_lo, 1)
            r = Q_END // RING - 2
            split(r, RING - 1)
            split(r, RING, more_hi, more_lo)
            residual(DT // 2 - 2, 1)
            split(r, RING + 1, more_hi, more_lo)
            statistics(DT // 2 - 2, 1)
            split(r, RING + 2, more_hi, more_lo)
            split(r, RING + 3, more_hi, more_lo)
            dve.wait_ge(z_stats, DT - 2)
            scaled(EARLY, slice(0, (DT - 2) * P))
            for m in range(2):
                part_residual(DT - 1 + m, m, LATE)

            deviations(1, LATE)
            late = slice(LATE[0], XT + 1)
            dve.scalar_tensor_tensor(out=rstd[3][:, late], in0=moments[:, late, 0], scalar=-1.0, in1=rstd[2][:, late],
                                     op0=ALU.mult, op1=ALU.mult).then_inc(shift_ready, 1)

            def normalise(t, cols):
                zt = z[:, t, cols]
                link(dve.scalar_tensor_tensor(out=zt, in0=zt, scalar=moments[:, t, 0:1], in1=gamma[:, cols],
                                              op0=ALU.subtract, op1=ALU.mult))
                dve.scalar_tensor_tensor(out=zt, in0=zt, scalar=rstd[2][:, t:t + 1], in1=beta[:, cols],
                                         op0=ALU.mult, op1=ALU.add).then_inc(normed, 1)

            normalise(LATE[0], slice(0, D))
            normalise(LATE[1], slice(0, D // 2))
            part_residual(DT + 1, 0, EARLY)
            part_residual(DT + 2, 1, EARLY)
            deviations(2, EARLY)
            for t in EARLY:
                ins = dve.tensor_scalar(shift_cols[:, t, 0:65:32], minus_one[:, 0:3], moments[:, t, 0:1], rstd[2][:, t:t + 1],
                                        ALU.mult, ALU.mult)
            ins.then_inc(shift_spread, 1)
            dve.wait_ge(z_stats, DT + 2)
            scaled(EARLY, slice((DT - 2) * P, D))
            dve.scalar_tensor_tensor(out=rstd[3][:, 0:1], in0=moments[:, 0:1, 0], scalar=-1.0, in1=rstd[2][:, 0:1],
                                     op0=ALU.mult, op1=ALU.mult).then_inc(shift_ready, 1)
            dve.wait_ge(shift_ready, 2)
            first = slice(0, D // 2)
            link(dve.scalar_tensor_tensor(out=bracket[:, :], in0=gamma[:, first], scalar=rstd[3][:, 0:1], in1=beta[:, first],
                                          op0=ALU.mult, op1=ALU.add))
            dve.wait_ge(shift_hi, 1)
            dve.tensor_tensor(shift_rows[64:66, :, :].rearrange("p t n -> p (t n)"), ps[64:66, 0, 0:TE],
                              f32(shift_rows[64:66, :, :].rearrange("p t n -> p (t n)")), ALU.subtract).then_inc(shift_lo, 1)
            dve.wait_ge(z_scaled, 2)
            for n in range(2 * len(EARLY)):
                t, cols = n // 2, slice(n % 2 * D // 2, (n % 2 + 1) * D // 2)
                if n:
                    dve.wait_ge(bracket_ready, n)
                rest = ps[:, 2 * n:2 * n + 2, :] if n else bracket[:, :].rearrange("p (b n) -> p b n", b=2)
                dve.scalar_tensor_tensor(out=z[:, t, cols].rearrange("p (b n) -> p b n", b=2), in0=z[:, t, cols].rearrange("p (b n) -> p b n", b=2),
                                         scalar=rstd[2][:, t:t + 1], in1=rest, op0=ALU.mult, op1=ALU.add)\
                    .then_inc(y_ready, 1)

        @block.tensor
        def _(pe):
            def products(out_halves, hi, lo, xs_h, xs_l, first, last):
                n = 0
                terms = ((hi, xs_h), (hi, xs_l), (lo, xs_h))
                for w, xs in terms:
                    for h in range(2):
                        ins = pe.matmul(out_halves[h], w, xs[h], start=first and n == 0, stop=last and n == 2)
                    n += 1
                return ins

            def chunk(r, j, p, rhs_h, rhs_l, k0, ks):
                pe.wait_ge(weight_lo_ready, r * RING + (j + 1))
                for c in range(CK):
                    k = k0 + c
                    ins = products([ps[:, 2 * p + h, 0:TH] for h in range(2)], weight_hi[:, j % RING, c, :], weight_lo[:, j % RING, c, :],
                                   [rhs_h[:, k, h * TH:(h + 1) * TH] for h in range(2)],
                                   [rhs_l[:, k, h * TH:(h + 1) * TH] for h in range(2)], k == 0, k == ks - 1)
                ins.then_inc(chunk_done, 1)

            def x_tile(r, j, p):
                for c in range(DT // CK):
                    chunk(r, j + c, p, xh, xl, c * CK, DT)

            def bank_of(s):
                wait(pe, setup_taken, s - 3)
                return setup_bank(s)

            def turn_x(s):
                c, t, n = x_step(s)
                pe.wait_ge(x_landed[c], 32)
                b = bank_of(s)
                for k in range(CK):
                    ins = pe.transpose(b[:, k * n:(k + 1) * n], x_rows[0:n, t, (CK * c + k) * P:(CK * c + k + 1) * P], ident[0:n, 0:n])
                ins.then_inc(setup_turned, 1)

            def turn_params():
                pe.wait_ge(consts_landed, 16 * 8)
                b = bank_of(X_BANKS)
                pe.transpose(b[:, 0:P], chan_rows[:, :], ident[:, :])
                nb = 2 * DT + PT_
                pe.transpose(b[:, P:P + nb], bias_rows[:, :], ident[0:nb, 0:nb]).then_inc(setup_turned, 1)

            def first_chunk(q):
                c, m = divmod(q, 2)
                if q == PER_GATE - 1:
                    turn_params()
                if m == 0:
                    pe.wait_ge(setup_taken, (c + 1) * (XT + 1))
                chunk(0, q, m, xh, xl, c * CK, DT)

            pe.wait_ge(ident_landed, 16)
            setup_order(turn_x, first_chunk, TURNED_BEFORE)
            pe.wait_ge(states_landed, 48)
            for s, state, rows, ks in ((1, conv_state, NSEQ * CH, range(DT)), (2, h_state, NSEQ, range(DT)),
                                       (3, pool_state, NSEQ * HIST, range(4)), (4, pool_state, NSEQ * HIST, range(4, 8))):
                b = bank_of(X_BANKS + s)
                for n, k in enumerate(ks):
                    ins = pe.transpose(b[:, n * rows:(n + 1) * rows], state[:, k * P:(k + 1) * P], ident[0:rows, 0:rows])
                ins.then_inc(setup_turned, 1)

            def gate(i):
                for m in range(2):
                    wait(pe, gate_tanh_ready, i * 2 + (m - 1))
                    x_tile(rounds(i, PER_GATE, Q_GATE), 4 * m, m)

            with pe.Fori(1, DT // 2) as i:
                gate(i)

            def pool_group(g):
                r = rounds(g, PER_POOL, Q_POOL)
                for u in range(2):
                    pe.wait_ge(gate_tanh_ready, DT - 1 + u)
                    wait(pe, ya_ready, g * 2 + (u - 1))
                    x_tile(r, 4 * u, u)
                pe.wait_ge(setup_taken, SETUP_BANKS)
                wait(pe, pool_silu_ready, g * 2 - 1)
                x_tile(r, 8, 2)
                pe.wait_ge(pw_lo_ready, g + 1)
                pe.wait_ge(diff_lo, g * 2 + 2)
                for j in range(2):
                    for k in range(2):
                        ins = products([ps[:, 2 * j + h, 0:TH] for h in range(2)], pw_hi[:, k, j * P:(j + 1) * P], pw_lo[:, k, j * P:(j + 1) * P],
                                       [dfh[:, k, h * TH:(h + 1) * TH] for h in range(2)],
                                       [dfl[:, k, h * TH:(h + 1) * TH] for h in range(2)], k == 0, k == 1)
                    ins.then_inc(mixed_done, 1)
                wait(pe, pool_silu_ready, g * 2)
                x_tile(r, 12, 3)

            pool_group(0)
            with pe.Fori(1, GROUPS) as g:
                pool_group(g)

            def proj_a(i):
                r = rounds(i, PER_PROJA, Q_PROJA)
                for m in range(2):
                    pe.wait_ge(ya_ready, PT_ - 1 + m)
                    wait(pe, ma_tanh_ready, i * 2 + (m - 1))
                    x_tile(r, 4 * m, m)
                pe.wait_ge(ya_lo, PT_)
                for m in range(2):
                    wait(pe, part_ready, i * 2 + (m - 1))
                    for c in range(2):
                        chunk(r, 8 + 2 * m + c, 2 + m, yah, yal, c * CK, PT_)

            proj_a(0)
            with pe.Fori(1, DT // 2) as i:
                proj_a(i)

            def lru(n):
                r = rounds(n, PER_LRU, Q_LRU)
                pe.wait_ge(ma_tanh_ready, DT)
                wait(pe, conv_ext_ready, n)
                x_tile(r, 0, 0)
                wait(pe, gb_silu_ready, n)
                x_tile(r, 4, 1)
                pe.wait_ge(part_ready, DT)
                wait(pe, i_ready, n)
                pe.wait_ge(conv_lo, n + 1)
                pe.wait_ge(small_lo_ready, n + 1)
                for k in range(2):
                    ins = products([ps[:, 4 + 2 * k + h, 0:XEH] for h in range(2)], small_hi[:, k, :], small_lo[:, k, :],
                                   [conv_x_hi[:, h * XEH:(h + 1) * XEH] for h in range(2)],
                                   [conv_x_lo[:, h * XEH:(h + 1) * XEH] for h in range(2)], True, True)
                ins.then_inc(lru_done, 1)

            lru(0)
            with pe.Fori(1, BLOCKS) as n:
                lru(n)

            def proj_b(i):
                r = rounds(i, PER_PROJB, Q_PROJB)
                for m in range(2):
                    pe.wait_ge(gb_silu_ready, BLOCKS)
                    wait(pe, merge_ready, i * 2 + (m - 1))
                    for c in range(DT // CK):
                        pe.wait_ge(yb_lo, (c + 1) * CK)
                        chunk(r, 4 * m + c, m, ybh, ybl, c * CK, DT)

            for j, (m, c) in enumerate(PROJB_FIRST):
                pe.wait_ge(gb_silu_ready if m else conv_ext_ready, BLOCKS)
                pe.wait_ge(yb_lo, (c + 1) * CK)
                chunk(Q_PROJB // RING, j, m, ybh, ybl, c * CK, DT)
            pe.wait_ge(h_kept, BLOCKS)
            flat = lambda t: t[:, :, :].rearrange("p s j -> p (s j)")
            tiles = [(0, flat(pool_rows), HIST * PT_ + c * P, c) for c in range(4)]
            tiles += [(1, flat(pool_rows), 0, 0), (1, flat(h_rows), 0, 1), (1, flat(h_rows), DT, 2)]
            tiles += [(2, flat(conv_rows), CH * DT + c * P, c) for c in range(3)] + [(2, flat(conv_rows), 0, 3)]
            for b, src, first, c in tiles:
                ins = pe.transpose(ps[:, 4 + b, c * P:(c + 1) * P], src[:, first:first + P], ident[:, :])
            ins.then_inc(rows_turned, 1)
            with pe.Fori(1, DT // 2) as i:
                proj_b(i)

            def turn(i, m):
                pe.wait_ge(out_copied, i * 2 + (m + 1))
                pe.wait_ge(rows_ready, 3)
                wait(pe, z_added, i * 2 + (m - 1))
                for t in range(XT):
                    pe.transpose(ps[:, 4 + 2 * m, t * P:(t + 1) * P], out_sb[m][:, t * P:(t + 1) * P], ident[:, :])
                pe.transpose(ps[0:SAMP, 5 + 2 * m, 0:P], out_sb[m][:, SEQ:T], ident[:, :]).then_inc(out_turned, 1)

            def project(i, before):
                r = rounds(i, PER_OUT, Q_OUT)
                for m in range(2):
                    pe.wait_ge(merge_ready, DT - 1 + m)
                    wait(pe, out_copied, i * 2 + (m - 1))
                    for c in range(DT // CK):
                        pe.wait_ge(merged_lo, (c + 1) * CK)
                        chunk(r, 4 * m + c, m, xh, xl, c * CK, DT)
                        if c == 0 and (m or before is not None):
                            turn(*((i, 0) if m else (before, 1)))

            project(0, None)
            with pe.Fori(1, DT // 2 - 1) as i:
                project(i, i - 1)

            def part_turn(n, m, tiles):
                pe.wait_ge(out_copied, n)
                pe.wait_ge(z_added, n - 2)
                for t in tiles:
                    if t < XT:
                        ins = pe.transpose(ps[:, 4 + 2 * m, t * P:(t + 1) * P], out_sb[m][:, t * P:(t + 1) * P], ident[:, :])
                    else:
                        ins = pe.transpose(ps[0:SAMP, 5 + 2 * m, 0:P], out_sb[m][:, SEQ:T], ident[:, :])
                ins.then_inc(out_turned, 1)

            def part_chunk(j, bank, tokens, turn_then=None):
                hi, lo = (weight_hi, weight_lo) if j < RING else (more_hi, more_lo)
                c = j % RING
                for kk in range(CK):
                    k = c * CK + kk
                    for n, (w, x) in enumerate(((hi, xh), (hi, xl), (lo, xh))):
                        ins = pe.matmul(ps[:, bank, 0:tokens.stop - tokens.start], w[:, c, kk, :], x[:, k, tokens],
                                        start=k == 0 and n == 0, stop=k == DT - 1 and n == 2)
                    if kk == 1 and turn_then:
                        part_turn(*turn_then)
                return ins

            r = Q_END // RING - 2
            for j in range(PER_OUT):
                m = j // RING
                if j % RING == 0:
                    pe.wait_ge(out_copied, DT - 3 + m)
                pe.wait_ge(weight_lo_ready, r * RING + (j + 1))
                part_chunk(j, 2 * m, slice(TE, T), (DT - 1, 0, LATE) if j == RING else None).then_inc(chunk_done, 1)
                if j == 0:
                    turn(DT // 2 - 2, 1)
            for j in range(PER_OUT):
                m = j // RING
                ins = part_chunk(j, 2 * m + 1, slice(0, TE), {0: (DT, 1, LATE), RING: (DT + 1, 0, EARLY)}.get(j))
                if j % RING == RING - 1:
                    ins.then_inc(early_done, 1)
            part_turn(DT + 2, 1, EARLY)
            pe.wait_ge(shift_spread, 1)
            for t in EARLY:
                ins = pe.transpose(ps[0:SHIFT_ROWS, 0, t * P:(t + 1) * P], shift_cols[:, t, :], ident[:, :])
            ins.then_inc(shift_turned, 1)
            pe.wait_ge(shift_lo, 1)
            pe.wait_ge(scale_lo, 1)
            pe.wait_ge(z_added, DT + 2)
            for t in EARLY:
                for b in range(0 if t else D // 1024, D // 512):
                    ins = pe.matmul(ps[:, t * (D // 512) + b, :], shift_rows[0:SHIFT_ROWS, t, :], scale_rows[0:SHIFT_ROWS, b * 512:(b + 1) * 512],
                                    start=True, stop=True)
                    if b % 2:
                        ins.then_inc(bracket_ready, 1)


def kernel(**inputs):
    import numpy as np
    import concourse.bacc as bacc
    from concourse.bass_utils import run_bass_kernel_spmd

    nc = bacc.Bacc("TRN2", target_bir_lowering=False, num_devices=1)
    arrays = {f"in_{n}": np.ascontiguousarray(inputs[n]) for n in INPUTS}
    hist = inputs["state_pool"].shape[2]
    arrays["identity"] = np.eye(P, dtype=np.float32)
    arrays["reciprocals"] = np.broadcast_to((1.0 / np.arange(1, hist + 1)).astype(np.float32), (P, hist)).copy()
    aps = {n: nc.dram_tensor(n, v.shape, mybir.dt.from_np(v.dtype), kind="ExternalInput").ap() for n, v in arrays.items()}
    names = ("x_prompt", "x_sample", "state_pool", "state_conv", "state_h")
    prompt, sample, spool, sconv, sh = (inputs[n].shape for n in names)
    shapes = [prompt, sample,
              (spool[0], prompt[0], *spool[2:]), (sconv[0], prompt[0], *sconv[2:]), (sh[0], prompt[0], sh[2]),
              spool, sconv, sh]
    outs = [nc.dram_tensor(f"out_{i}", s, F32, kind="ExternalOutput").ap() for i, s in enumerate(shapes)]
    build(nc, {n: aps[f"in_{n}"] for n in INPUTS}, aps, outs)
    r = run_bass_kernel_spmd(nc, [arrays], core_ids=[0])
    return tuple(r.results[0][f"out_{i}"] for i in range(len(outs)))
```
